# Optimizing a Trainium2 kernel written in Bass

```python
import math, functools
import jax, jax.numpy as jnp
from jax import lax
import numpy as np

D_MODEL = 1024
BATCH = 1
SEQ = 256
DEPTH = 1
DEC_BATCH = 8
DEC_SEQ = 8
PAST_LEN = 2048
PAGE_SIZE = 128

N_META = 16
HEAD_DIM = 64
A_WIDTH = D_MODEL // 2
A_HEADS = A_WIDTH // HEAD_DIM
B_WIDTH = D_MODEL // 2
B_HEADS = B_WIDTH // HEAD_DIM
W_LORA = 64
A_LORA = 64
G_LORA = 128
A_PROJ = 3 * A_WIDTH + W_LORA + A_LORA + G_LORA
B_PROJ = 3 * B_WIDTH + B_HEADS
P_TOTAL = A_PROJ + B_PROJ + 2 * D_MODEL
N_GROUPS = 4
EXP_PER_GROUP = 8
N_EXPERTS = N_GROUPS * EXP_PER_GROUP
TOP_K_IN_GROUP = 2
EXPERT_FF = D_MODEL // 4
Q_BLOCK = 128
RMS_EPS = 1e-6
GN_EPS = 64e-5
NEG_INF = -1e30

kernel_name = 'rwkv7_fox_gated_hier_moe_step'

def rms_norm(x, w):
    xf = x.astype(jnp.float32)
    y = xf * lax.rsqrt(jnp.mean(xf * xf, axis=-1, keepdims=True) + RMS_EPS)
    return (y * w.astype(jnp.float32)).astype(x.dtype)

def rwkv_scan(s0, r, w, k, v, kk, a):
    tm = lambda u: jnp.moveaxis(u.astype(jnp.float32), 1, 0)
    xs = (tm(r), tm(w), tm(k), tm(v), tm(kk), tm(kk * a))

    def step(s, inp):
        r_t, w_t, k_t, v_t, kk_t, b_t = inp
        sa = jnp.einsum('bhvk,bhk->bhv', s, kk_t)
        s = s * w_t[:, :, None, :] - sa[..., None] * b_t[:, :, None, :] + v_t[..., None] * k_t[:, :, None, :]
        return s, jnp.einsum('bhvk,bhk->bhv', s, r_t)

    s_fin, o = lax.scan(step, s0.astype(jnp.float32), xs)
    return s_fin, jnp.moveaxis(o, 0, 1)

def rwkv_branch(za, shift0, s0, p):
    b, t, _ = za.shape
    za_prev = jnp.concatenate([shift0[:, None, :].astype(za.dtype), za[:, :-1]], axis=1)
    zs = za + (za_prev - za) * p['mu']
    i1, i2, i3 = A_WIDTH, 2 * A_WIDTH, 3 * A_WIDTH
    i4 = i3 + W_LORA
    i5 = i4 + A_LORA
    r, k, v = zs[..., :i1], zs[..., i1:i2], zs[..., i2:i3]
    wl, al, gl = zs[..., i3:i4], zs[..., i4:i5], zs[..., i5:]
    log_w = -math.exp(-0.5) * jax.nn.sigmoid((p['w0'] + jnp.tanh(wl) @ p['w2']).astype(jnp.float32))
    a = jax.nn.sigmoid((p['a0'] + al @ p['a2']).astype(jnp.float32))
    g = (jax.nn.sigmoid(gl) @ p['g2']).astype(jnp.float32)
    heads = lambda u: u.astype(jnp.float32).reshape(b, t, A_HEADS, HEAD_DIM)
    kk = heads(k * p['k_k'])
    kk = kk * lax.rsqrt(jnp.maximum(jnp.sum(kk * kk, axis=-1, keepdims=True), 1e-24))
    k_mod = k.astype(jnp.float32) * (1.0 + (a - 1.0) * p['k_a'].astype(jnp.float32))
    rh, kh, vh, ah, wh = heads(r), heads(k_mod), heads(v), heads(a), jnp.exp(heads(log_w))
    s_fin, o = rwkv_scan(s0, rh, wh, kh, vh, kk, ah)
    mean = jnp.mean(o, axis=-1, keepdims=True)
    var = jnp.mean(jnp.square(o - mean), axis=-1, keepdims=True)
    o = (o - mean) * lax.rsqrt(var + GN_EPS)
    o = o * p['lnx_w'].astype(jnp.float32).reshape(A_HEADS, HEAD_DIM) + p['lnx_b'].astype(jnp.float32).reshape(A_HEADS, HEAD_DIM)
    bonus = jnp.sum(rh * kh * p['r_k'].astype(jnp.float32), axis=-1, keepdims=True) * vh
    out = ((o + bonus).reshape(b, t, A_WIDTH) * g).astype(za.dtype)
    return out, s_fin, za[:, -1]

def fox_features(zb, f_bias, q_norm, k_norm):
    b, t, _ = zb.shape
    heads = lambda u: u.reshape(b, t, B_HEADS, HEAD_DIM)
    q = rms_norm(heads(zb[..., :B_WIDTH]), q_norm)
    k = rms_norm(heads(zb[..., B_WIDTH:2 * B_WIDTH]), k_norm)
    v = heads(zb[..., 2 * B_WIDTH:3 * B_WIDTH])
    log_f = jax.nn.log_sigmoid((zb[..., 3 * B_WIDTH:] + f_bias).astype(jnp.float32))
    return q, k, v, log_f

def fox_attend(q, c_q, pos_q, k, v, c_k, pos_k):
    s = jnp.einsum('bqhd,bkhd->bhqk', q.astype(jnp.float32), k.astype(jnp.float32)) * (HEAD_DIM ** -0.5)
    s = s + jnp.swapaxes(c_q, 1, 2)[:, :, :, None] - jnp.swapaxes(c_k, 1, 2)[:, :, None, :]
    s = jnp.where(pos_k[None, :] <= pos_q[:, None], s, NEG_INF)
    pr = jax.nn.softmax(s, axis=-1)
    return jnp.einsum('bhqk,bkhd->bqhd', pr, v.astype(jnp.float32))

def fox_prompt(q, k, v, log_f):
    b, L = q.shape[0], q.shape[1]
    c = jnp.cumsum(log_f, axis=1)
    pos = jnp.arange(L)
    o_meta = fox_attend(q[:, :N_META], c[:, :N_META], pos[:N_META],
                        k[:, :N_META], v[:, :N_META], c[:, :N_META], pos[:N_META])
    n_blk = (L - N_META) // Q_BLOCK

    def one_block(i):
        start = N_META + i * Q_BLOCK
        qb = lax.dynamic_slice_in_dim(q, start, Q_BLOCK, axis=1)
        cb = lax.dynamic_slice_in_dim(c, start, Q_BLOCK, axis=1)
        return fox_attend(qb, cb, start + jnp.arange(Q_BLOCK), k, v, c, pos)

    o_blk = lax.map(one_block, jnp.arange(n_blk))
    o_real = jnp.moveaxis(o_blk, 0, 1).reshape(b, n_blk * Q_BLOCK, B_HEADS, HEAD_DIM)
    return jnp.concatenate([o_meta, o_real], axis=1)

def fox_sample(q, k, v, log_f, k_past, v_past, lf_past):
    past, t = k_past.shape[1], q.shape[1]
    lf_past = lf_past.astype(jnp.float32)
    r_past = lax.cumsum(lf_past, axis=1, reverse=True) - lf_past
    c_new = jnp.cumsum(log_f, axis=1)
    keys = jnp.concatenate([k_past, k.astype(k_past.dtype)], axis=1)
    vals = jnp.concatenate([v_past, v.astype(v_past.dtype)], axis=1)
    c_k = jnp.concatenate([-r_past, c_new], axis=1)
    return fox_attend(q, c_new, past + jnp.arange(t), keys, vals, c_k, jnp.arange(past + t))

def token_mixer(h, shift0, s0, attend, p):
    xn = rms_norm(h, p['ln1'])
    z = xn @ p['w_in']
    c1 = A_PROJ
    c2 = c1 + B_PROJ
    c3 = c2 + D_MODEL
    za, zb, ga, gb = z[..., :c1], z[..., c1:c2], z[..., c2:c3], z[..., c3:]
    oa, s_new, shift_new = rwkv_branch(za, shift0, s0, p)
    q, k, v, log_f = fox_features(zb, p['f_bias'], p['q_norm'], p['k_norm'])
    ob = attend(q, k, v, log_f)
    b, t, _ = h.shape
    ob = ob.reshape(b, t, B_WIDTH).astype(h.dtype)
    merged = jax.nn.sigmoid(ga) * (oa @ p['proj_a']) + jax.nn.sigmoid(gb) * (ob @ p['proj_b'])
    return (merged @ p['w_out']).astype(h.dtype), (k, v, log_f, s_new, shift_new)

def hier_moe(x, router_grp, router_exp, w1, w3, w2):
    shp = x.shape
    xt = x.reshape(-1, D_MODEL)
    n_tok = xt.shape[0]
    grp_prob = jax.nn.softmax((xt @ router_grp).astype(jnp.float32), axis=-1)
    gp, gi = lax.top_k(grp_prob, 1)
    exp_logits = (xt @ router_exp).astype(jnp.float32).reshape(n_tok, N_GROUPS, EXP_PER_GROUP)
    sel = jnp.take_along_axis(exp_logits, gi[:, :, None], axis=1)[:, 0]
    ev, ei = lax.top_k(sel, TOP_K_IN_GROUP)
    ew = jax.nn.softmax(ev, axis=-1) * gp
    eid = gi * EXP_PER_GROUP + ei
    combine = jnp.sum(jax.nn.one_hot(eid, N_EXPERTS, dtype=jnp.float32) * ew[..., None], axis=1)
    y = jnp.zeros((n_tok, D_MODEL), jnp.float32)
    for e in range(N_EXPERTS):
        hid = jax.nn.silu(xt @ w1[e]) * (xt @ w3[e])
        y = y + combine[:, e:e + 1] * (hid @ w2[e]).astype(jnp.float32)
    return y.astype(x.dtype).reshape(shp)

def setup_inputs(seed: int = 0) -> dict:
    key = jax.random.key(seed)
    keys = list(jax.random.split(key, 48))
    f32 = jnp.float32

    def nrm(shape, scale):
        return jax.random.normal(keys.pop(), shape, f32) * scale

    def gain(shape):
        return 1.0 + nrm(shape, 0.02)

    n_pages = PAST_LEN // PAGE_SIZE
    n_used = DEC_BATCH * n_pages
    n_phys = n_used + max(1, n_used // 4)
    f_center = jnp.linspace(1.0, 4.0, B_HEADS).astype(f32)
    inp = {}
    inp['x_prompt'] = nrm((BATCH, SEQ, D_MODEL), 1.0)
    inp['x_sample'] = nrm((DEC_BATCH, DEC_SEQ, D_MODEL), 1.0)
    inp['cache_k'] = nrm((DEPTH, n_phys, PAGE_SIZE, B_HEADS, HEAD_DIM), 1.0)
    inp['cache_v'] = nrm((DEPTH, n_phys, PAGE_SIZE, B_HEADS, HEAD_DIM), 1.0)
    inp['cache_logf'] = jax.nn.log_sigmoid(f_center + nrm((DEPTH, n_phys, PAGE_SIZE, B_HEADS), 1.0))
    inp['state_rwkv'] = nrm((DEPTH, DEC_BATCH, A_HEADS, HEAD_DIM, HEAD_DIM), 0.3)
    inp['state_shift'] = nrm((DEPTH, DEC_BATCH, A_PROJ), 1.0)
    inp['page_table'] = jax.random.permutation(keys.pop(), n_phys)[:n_used].reshape(DEC_BATCH, n_pages).astype(jnp.int32)
    inp['meta_tokens'] = nrm((N_META, D_MODEL), 1.0)
    inp['ln1_w'] = gain((DEPTH, D_MODEL))
    inp['w_in'] = nrm((DEPTH, D_MODEL, P_TOTAL), D_MODEL ** -0.5)
    inp['rwkv_mu'] = jax.random.uniform(keys.pop(), (DEPTH, A_PROJ), f32)
    inp['rwkv_w0'] = nrm((DEPTH, A_WIDTH), 0.5)
    inp['rwkv_w2'] = nrm((DEPTH, W_LORA, A_WIDTH), 0.5 * W_LORA ** -0.5)
    inp['rwkv_a0'] = nrm((DEPTH, A_WIDTH), 0.1)
    inp['rwkv_a2'] = nrm((DEPTH, A_LORA, A_WIDTH), 0.5 * A_LORA ** -0.5)
    inp['rwkv_g2'] = nrm((DEPTH, G_LORA, A_WIDTH), G_LORA ** -0.5)
    inp['rwkv_k_k'] = 0.85 + nrm((DEPTH, A_WIDTH), 0.05)
    inp['rwkv_k_a'] = 1.0 + nrm((DEPTH, A_WIDTH), 0.05)
    inp['rwkv_r_k'] = nrm((DEPTH, A_HEADS, HEAD_DIM), 0.1)
    inp['rwkv_lnx_w'] = gain((DEPTH, A_WIDTH))
    inp['rwkv_lnx_b'] = nrm((DEPTH, A_WIDTH), 0.02)
    inp['fox_q_norm'] = gain((DEPTH, HEAD_DIM))
    inp['fox_k_norm'] = gain((DEPTH, HEAD_DIM))
    inp['fox_f_bias'] = f_center + nrm((DEPTH, B_HEADS), 0.05)
    inp['proj_a'] = nrm((DEPTH, A_WIDTH, D_MODEL), A_WIDTH ** -0.5)
    inp['proj_b'] = nrm((DEPTH, B_WIDTH, D_MODEL), B_WIDTH ** -0.5)
    inp['w_out'] = nrm((DEPTH, D_MODEL, D_MODEL), D_MODEL ** -0.5)
    inp['ln2_w'] = gain((DEPTH, D_MODEL))
    inp['router_grp'] = nrm((DEPTH, D_MODEL, N_GROUPS), D_MODEL ** -0.5)
    inp['router_exp'] = nrm((DEPTH, D_MODEL, N_EXPERTS), D_MODEL ** -0.5)
    inp['exp_w1'] = nrm((DEPTH, N_EXPERTS, D_MODEL, EXPERT_FF), D_MODEL ** -0.5)
    inp['exp_w3'] = nrm((DEPTH, N_EXPERTS, D_MODEL, EXPERT_FF), D_MODEL ** -0.5)
    inp['exp_w2'] = nrm((DEPTH, N_EXPERTS, EXPERT_FF, D_MODEL), EXPERT_FF ** -0.5)
    inp['ln_f'] = gain((D_MODEL,))
    return inp

def reference(x_prompt, x_sample, cache_k, cache_v, cache_logf, state_rwkv, state_shift, page_table,
              meta_tokens, ln1_w, w_in, rwkv_mu, rwkv_w0, rwkv_w2, rwkv_a0, rwkv_a2, rwkv_g2,
              rwkv_k_k, rwkv_k_a, rwkv_r_k, rwkv_lnx_w, rwkv_lnx_b, fox_q_norm, fox_k_norm, fox_f_bias,
              proj_a, proj_b, w_out, ln2_w, router_grp, router_exp, exp_w1, exp_w3, exp_w2, ln_f):
    b_p = x_prompt.shape[0]
    b_s = x_sample.shape[0]
    n_pages = page_table.shape[1]
    past = n_pages * PAGE_SIZE
    meta = jnp.broadcast_to(meta_tokens[None].astype(x_prompt.dtype), (b_p, N_META, D_MODEL))
    hp = jnp.concatenate([meta, x_prompt], axis=1)
    hs = x_sample
    out_p = ([], [], [], [], [])
    out_s = ([], [], [], [], [])
    for l in range(DEPTH):
        p = {'ln1': ln1_w[l], 'w_in': w_in[l], 'mu': rwkv_mu[l], 'w0': rwkv_w0[l], 'w2': rwkv_w2[l],
             'a0': rwkv_a0[l], 'a2': rwkv_a2[l], 'g2': rwkv_g2[l], 'k_k': rwkv_k_k[l], 'k_a': rwkv_k_a[l],
             'r_k': rwkv_r_k[l], 'lnx_w': rwkv_lnx_w[l], 'lnx_b': rwkv_lnx_b[l], 'q_norm': fox_q_norm[l],
             'k_norm': fox_k_norm[l], 'f_bias': fox_f_bias[l], 'proj_a': proj_a[l], 'proj_b': proj_b[l],
             'w_out': w_out[l]}
        shift0 = jnp.zeros((b_p, A_PROJ), hp.dtype)
        s0 = jnp.zeros((b_p, A_HEADS, HEAD_DIM, HEAD_DIM), jnp.float32)
        mix_p, st_p = token_mixer(hp, shift0, s0, fox_prompt, p)
        hp = hp + mix_p
        k_past = cache_k[l][page_table].reshape(b_s, past, B_HEADS, HEAD_DIM)
        v_past = cache_v[l][page_table].reshape(b_s, past, B_HEADS, HEAD_DIM)
        lf_past = cache_logf[l][page_table].reshape(b_s, past, B_HEADS)
        attend_s = functools.partial(fox_sample, k_past=k_past, v_past=v_past, lf_past=lf_past)
        mix_s, st_s = token_mixer(hs, state_shift[l], state_rwkv[l], attend_s, p)
        hs = hs + mix_s
        for lst, arr in zip(out_p, st_p):
            lst.append(arr)
        for lst, arr in zip(out_s, st_s):
            lst.append(arr)
        if l == DEPTH - 1:
            hp = hp[:, N_META:]
        hp = hp + hier_moe(rms_norm(hp, ln2_w[l]), router_grp[l], router_exp[l], exp_w1[l], exp_w3[l], exp_w2[l])
        hs = hs + hier_moe(rms_norm(hs, ln2_w[l]), router_grp[l], router_exp[l], exp_w1[l], exp_w3[l], exp_w2[l])
    y_prompt = rms_norm(hp, ln_f)
    y_sample = rms_norm(hs, ln_f)
    k_p, v_p, lf_p, rw_p, sh_p = (jnp.stack(a, axis=0) for a in out_p)
    k_s, v_s, lf_s, rw_s, sh_s = (jnp.stack(a, axis=0) for a in out_s)
    return (y_prompt, y_sample, k_p, v_p, lf_p, rw_p, sh_p, k_s, v_s, lf_s, rw_s, sh_s)


_drawn_inputs = setup_inputs


def setup_inputs(seed=0):
    import zlib

    import numpy as np

    out = dict(_drawn_inputs(seed))
    spreads = {}
    factors = {'rwkv_k_k': 17.218,
     'rwkv_lnx_w': 8.0,
     'rwkv_lnx_b': 16.571,
     'fox_q_norm': 33.203,
     'ln_f': 7.503,
     'ln2_w': 4.8}
    for name, (base, spread) in spreads.items():
        noise = np.random.default_rng([zlib.crc32(name.encode()), seed]).standard_normal(out[name].shape)
        drawn = base * np.exp(spread * noise) if base else spread * noise
        out[name] = __import__('jax').numpy.asarray(drawn.astype(out[name].dtype))
    for name, factor in factors.items():
        out[name] = (out[name] * factor).astype(out[name].dtype)
    return out
```

```python
import math
import concourse.bass as bass
from concourse import mybir
from contextlib import ExitStack

DM, SEQ, NMETA, HD = 1024, 256, 16, 64
DB, DS = 8, 8
PAGE, NPAGES = 128, 16
AW = BW = DM // 2
NH = AW // HD
NPAIR = NH // 2
LORA, GL = 64, 128
AP_ = 3 * AW + 2 * LORA + GL
NG, EPG, FF = 4, 8, 256
NE = NG * EPG
LP = NMETA + SEQ
NS = DB * DS
T = LP + NS
P = 128
KT = DM // P
ROWS = [P, P, T - 2 * P]
NT = len(ROWS)
ATILES = AP_ // P
ZC = 1 + LP + DB * (1 + DS)
TW = NT * P
CH = 16
NCH = LP // CH
DECAY = math.exp(-0.5)
RMS_EPS, GN_EPS, NEG = 1e-6, 64e-5, -1e30
SLOTS, SLOT = 8, 2048
MU, W0, A0, KK, KA, RK, LNW, LNB = (0, ATILES, ATILES + 4, ATILES + 8, ATILES + 12, ATILES + 16,
                                    ATILES + 20, ATILES + 24)
NPRM = ATILES + 28


class Chain:

    def __init__(self, eng, sem):
        self.eng, self.sem, self.n, self.at = eng, sem, 0, 0

    def __call__(self, ins):
        ins.then_inc(self.sem, 1)
        self.n += 1
        self.eng.wait_ge(self.sem, self.at + self.n)


class Ring:

    def __init__(self):
        self.fills = [0] * SLOTS


class Space:

    def __init__(self, tensor, lo, hi):
        self.t, self.at, self.hi = tensor, lo, hi

    def __call__(self, *shape, parts=P):
        n = math.prod(shape)
        assert self.at + n <= self.hi, (self.at, n, self.hi)
        v = self.t[0:parts, self.at:self.at + n]
        self.at += n
        if len(shape) > 1:
            names = [f"d{i}" for i in range(len(shape))]
            v = v.rearrange(f"p ({' '.join(names)}) -> p {' '.join(names)}",
                            **{a: s for a, s in zip(names[1:], shape[1:])})
        return v


def bc(ap, axis, n):
    shape = list(ap.shape)
    return ap.unsqueeze(axis).broadcast_to(shape[:axis] + [n] + shape[axis:])


def build(nc, A, O):
    f32, i32 = mybir.dt.float32, mybir.dt.int32
    ALU, ACT, AX = mybir.AluOpType, mybir.ActivationFunctionType, mybir.AxisListType
    add, sub, mult, vmax, vmin = ALU.add, ALU.subtract, ALU.mult, ALU.max, ALU.min
    ctx = ExitStack()
    sems = {}

    def S(name):
        if name not in sems:
            sems[name] = nc.alloc_semaphore(name=name)
        return sems[name]

    def retire():
        old = [n for n in sems if not n.startswith("slot_full")]
        nc.clear_and_free_semaphores([sems.pop(n) for n in old])
        nc.all_engine_barrier()

    with ctx:
        NF = 53000
        arena = ctx.enter_context(nc.sbuf_tensor("arena", [P, NF], f32))
        pt_row = ctx.enter_context(nc.sbuf_tensor("pt_row", [1, DB * NPAGES], i32))
        pt_col = ctx.enter_context(nc.sbuf_tensor("pt_col", [P, 1], i32))
        bank = [ctx.enter_context(nc.psum_tensor(f"bank{i}", [P, 512], f32)) for i in range(8)]

        slot = [arena[:, i * SLOT:(i + 1) * SLOT] for i in range(SLOTS)]
        full = [S(f"slot_full{i}") for i in range(SLOTS)]
        keep = Space(arena, SLOTS * SLOT, NF)
        ident = keep(P)
        ones = keep(P)
        headones = keep(P)
        tri_tok = keep(P)
        same_head64 = None
        m_st = keep(NT, P)
        m_ts = keep(NT, P)
        m_si = keep(NT, P)
        cm2 = keep(2)
        cm8 = keep(DB)
        prm = keep(NPRM)
        lfb = keep(P)
        small = keep(256)
        xnT = keep(KT, T)
        obT = keep(NPAIR, T)
        q_all = keep(DB, NPAIR, 2 * DS)
        knT = keep(NPAIR, NS)
        newmask = keep(DB, NH, DS, parts=DS)
        base = keep.at

        ln_row = A["ln_rows"]

        sp1 = Space(arena, base, NF)
        za = sp1(ATILES, ZC)
        zb = sp1(NT, 3 * BW)
        qkT = sp1(2 * NPAIR, T)
        lf = sp1(NT, NH)
        causal01 = sp1(NT, LP)
        addmask = sp1(NT, LP)
        selneg = sp1(NH, P, parts=NH)
        cT = sp1(LP, parts=NH)
        mark1 = sp1.at
        xt = sp1(NT, DM)
        xn = sp1(NT, DM)
        lnb = sp1(DM)
        prm_rows = sp1(P)
        qkn = sp1(2, HD)
        fb = sp1(NH)
        wf = sp1(KT, NH)
        shift_tm = sp1(AP_, parts=DB)
        cn_tm = sp1(NH)
        cn8 = sp1(DB, NH, parts=DS)
        shift_out = sp1(AP_, parts=1 + DB)
        lft = sp1(4, NT, NH)
        junk = xn
        ss, ms, rt, rstd = (small[:, i * NT:(i + 1) * NT] for i in range(4))
        s16 = [sp1(NT, 2 * NH) for _ in range(4)]
        sq = xt

        A_vs = O["v_s"].rearrange("(b t) n -> b t n", t=DS)

        def page_numbers(sp, s, b):
            return [sp.value_load(pt_row[0:1, bass.ds(b * NPAGES + 4 * (s % 4) + n, 1)], min_val=0,
                                  max_val=A["ck"].shape[0] - 1) for n in range(4)]

        def load_pages(sp, s, pages):
            src = A["ck"] if s < 4 else A["cv"]
            for n in range(4):
                sp.dma_start(slot[s][:, n * BW:(n + 1) * BW],
                             src[bass.ds(pages[n], 1)].rearrange("a p n -> (a p) n")).then_inc(full[s], 16)

        def merge_load(n):
            if n >= 12:
                return A["w_out"][n - 12]
            dd, part = divmod(n, 3)
            return A["w_proj"][dd] if part == 2 else A["w_gate"][2 * dd + part]

        zslots = [(0, 1), (2, 3), (4, 5)]
        aslots = [6, 7, 0, 1, 2, 3, 4]

        with nc.Block("proj") as block:
            @block.sync
            def _(sp):
                sp.dma_start(xt[0:NMETA, 0, :], A["meta"]).then_inc(S("x_in0"), 16)
                sp.dma_start(xt[NMETA:P, 0, :], A["xp"][0:P - NMETA, :]).then_inc(S("x_in0"), 16)
                sp.dma_start(xt[:, 1, :], A["xp"][P - NMETA:2 * P - NMETA, :]).then_inc(S("x_in1"), 16)
                sp.dma_start(xt[0:NMETA, 2, :], A["xp"][2 * P - NMETA:SEQ, :]).then_inc(S("x_in2"), 16)
                sp.dma_start(xt[NMETA:ROWS[2], 2, :], A["xs"]).then_inc(S("x_in2"), 16)
                sp.dma_start(lnb, ln_row[0, :].partition_broadcast(P)).then_inc(S("ln_in"), 16)

                for c, pair in enumerate(zslots):
                    for half, s in enumerate(pair):
                        sp.dma_start(slot[s], A["w_zb"][c, half]).then_inc(full[s], 16)
                for c, s in enumerate(aslots):
                    if s < 6:
                        sp.wait_ge(S("zb_ps"), 3 * (s // 2) + 3)
                    sp.dma_start(slot[s], A["w_za"][c]).then_inc(full[s], 16)
                sp.wait_ge(S("pt_in"), 32)
                for s in (5, 6, 7, 0, 1, 2, 3, 4):
                    if s != 5:
                        sp.wait_ge(S("za_ps"), 2 * aslots.index(s) + 2)
                    load_pages(sp, s, page_numbers(sp, s, 0))

            @block.gpsimd
            def _(pool):
                ch = Chain(pool, S("pool_self"))

                def mask(ap, pattern, op, fill, basev, cmul):
                    ch(nc.gpsimd.affine_select(out=ap, in_=ap, compare_op=op, fill=fill, base=basev,
                                               pattern=pattern, channel_multiplier=cmul))
                ch(nc.gpsimd.memset(ident, 0.0))
                mask(ident, [[-1, P]], ALU.not_equal, 1.0, 0, 1)
                ch(nc.gpsimd.memset(ones, 1.0))
                pool.sem_inc(S("ident_ready"), 1)
                ch(nc.gpsimd.memset(za[:, :, 0:1], 0.0))
                ch(nc.gpsimd.memset(selneg, 0.0))
                mask(selneg, [[-1, NH], [0, P]], ALU.not_equal, -1.0, 0, 1)
                for m, fill0 in ((causal01, 1.0), (addmask, 0.0)):
                    ch(nc.gpsimd.memset(m, fill0))
                mask(causal01, [[-P, NT], [1, LP]], ALU.is_ge, 0.0, 0, -1)
                mask(addmask, [[P, NT], [-1, LP]], ALU.is_ge, NEG, 0, 1)
                for m in (m_st, m_ts, m_si):
                    ch(nc.gpsimd.memset(m, 1.0))
                    for j, w in ((0, CH), (1, CH), (2, DS)):
                        v = m[:, j, :].rearrange("p (c w) -> p c w", w=w)
                        mask(v, [[-w, P // w], [0, w]], ALU.is_ge, 0.0, 0, 1)
                        mask(v, [[w, P // w], [0, w]], ALU.is_ge, 0.0, w - 1, -1)
                    ch(nc.gpsimd.memset(m[0:CH, 2, 0:CH], 1.0))
                    v = m[:, 2, T - 2 * P:P]
                    ch(nc.gpsimd.memset(v, 0.0))
                mask(m_st, [[0, NT], [1, P]], ALU.is_gt, 0.0, 0, -1)
                mask(m_ts, [[0, NT], [-1, P]], ALU.is_gt, 0.0, 0, 1)
                mask(m_si, [[0, NT], [1, P]], ALU.is_ge, 0.0, 0, -1)
                ch(nc.gpsimd.memset(tri_tok, 1.0))
                mask(tri_tok, [[1, P]], ALU.is_gt, 0.0, 0, -1)
                ch(nc.gpsimd.memset(headones, 0.0))
                ch(nc.gpsimd.memset(headones[0:HD, 0:HD], 1.0))
                ch(nc.gpsimd.memset(headones[HD:P, HD:P], 1.0))
                ch(nc.gpsimd.memset(cm8, 1.0))
                mask(cm8, [[-DS, DB]], ALU.is_ge, 0.0, -CH, 1)
                mask(cm8, [[DS, DB]], ALU.is_ge, 0.0, CH + DS - 1, -1)
                cmg = small[:, 200:208].rearrange("p (g s) -> p g s", g=4)
                ch(nc.gpsimd.memset(cmg, 1.0))
                mask(cmg, [[-2 * CH, 4], [-CH, 2]], ALU.is_ge, 0.0, 0, 1)
                mask(cmg, [[2 * CH, 4], [CH, 2]], ALU.is_ge, 0.0, CH - 1, -1)
                ch(nc.gpsimd.tensor_tensor(cmg[:, 0:2, :], cmg[:, 0:2, :], cmg[:, 2:4, :], add))
                ch(nc.gpsimd.tensor_tensor(cm2, cmg[:, 0, :], cmg[:, 1, :], add))
                ch(nc.gpsimd.memset(newmask, 0.0))
                mask(newmask, [[0, DB], [0, NH], [1, DS]], ALU.is_ge, NEG, 0, -1)
                ch(nc.gpsimd.memset(q_all, 0.0))
                pool.sem_inc(S("masks_ready"), 1)

                pool.wait_ge(S("lf_ready"), 1)
                out = S("out_done")
                for dst, dst_s, src in ((O["lf_p"], O["lf_s"], lf),):
                    nc.gpsimd.dma_start(dst[0:P, :], src[:, 0, :]).then_inc(out, 16)
                    nc.gpsimd.dma_start(dst[P:2 * P, :], src[:, 1, :]).then_inc(out, 16)
                    nc.gpsimd.dma_start(dst[2 * P:LP, :], src[0:NMETA, 2, :]).then_inc(out, 16)
                    nc.gpsimd.dma_start(dst_s, src[NMETA:ROWS[2], 2, :]).then_inc(out, 16)
                pool.wait_ge(S("cn_ready"), 1)
                nc.gpsimd.dma_start(A["cn_dram"], cn_tm[NMETA:ROWS[2], :]).then_inc(S("cn_out"), 16)
                pool.wait_ge(S("cn_out"), 16)
                nc.gpsimd.dma_start(cn8, A["cn_dram"].rearrange("(b t) h -> t b h", t=DS)).then_inc(S("cn_in"), 16)
                pool.wait_ge(S("cn_in"), 16)
                ch(nc.gpsimd.tensor_tensor(newmask, newmask, bc(cn8, 3, DS), sub))
                pool.wait_ge(S("qk_ready"), 1)
                for (dst, dst_s), col in (((O["k_p"], O["k_s"]), BW), ((O["v_p"], O["v_s"]), 2 * BW)):
                    c = slice(col, col + BW)
                    nc.gpsimd.dma_start(dst[0:P, :], zb[:, 0, c]).then_inc(out, 16)
                    nc.gpsimd.dma_start(dst[P:2 * P, :], zb[:, 1, c]).then_inc(out, 16)
                    nc.gpsimd.dma_start(dst[2 * P:LP, :], zb[0:NMETA, 2, c]).then_inc(out, 16)
                    nc.gpsimd.dma_start(dst_s, zb[NMETA:ROWS[2], 2, c]).then_inc(out, 16)
                pool.wait_ge(S("shift_ready"), 1)
                nc.gpsimd.dma_start(O["shift_p"], shift_out[0:1, :]).then_inc(out, 16)
                nc.gpsimd.dma_start(O["shift_s"], shift_out[1:1 + DB, :]).then_inc(out, 16)
                pool.wait_ge(S("pt_in"), 32)
                pool.wait_ge(out, 16 * 14)

            @block.scalar
            def _(act):
                ch = Chain(act, S("act_self"))
                act.dma_start(prm_rows[0:NPRM, :], A["prm"]).then_inc(S("prm_in"), 16)
                act.dma_start(wf, A["w_f"]).then_inc(S("wf_in"), 16)
                act.dma_start(shift_tm, A["shift"]).then_inc(S("shift_in"), 16)
                act.dma_start(qkn, A["qkn"].partition_broadcast(P)).then_inc(S("fp_in"), 16)
                act.dma_start(fb, A["fb"].partition_broadcast(P)).then_inc(S("fp_in"), 16)
                act.dma_start(pt_row[:, :], A["pt"]).then_inc(S("pt_in"), 16)
                act.dma_start(pt_col[:, :], A["pt"].rearrange("a n -> n a")).then_inc(S("pt_in"), 16)
                act.wait_ge(S("stats_zeroed"), 1)
                for i, n in enumerate(ROWS):
                    act.wait_ge(S(f"x_in{i}"), 16 if i == 1 else 32)
                    nc.scalar.activation(junk[0:n, i, :], xt[0:n, i, :], ACT.Square,
                                         accum_out=ss[0:n, i:i + 1]).then_inc(S("ss_ready"), 1)
                act.wait_ge(S("ms_ready"), 1)
                nc.scalar.activation(rt, ms, ACT.Sqrt).then_inc(S("rt_ready"), 1)
                for i, n in enumerate(ROWS):
                    act.wait_ge(S("xT_ps"), 2 * i + 2)
                    nc.scalar.activation(xnT[:, 4:8, i * P:i * P + n],
                                         bank[2 * i + 1][:, :].rearrange("p (k t) -> p k t", k=4)[:, :, 0:n],
                                         ACT.Copy).then_inc(S("xnT_b"), 1)
                for c in range(3):
                    for i, n in enumerate(ROWS):
                        q = 3 * c + i
                        act.wait_ge(S("zb_ps"), q + 1)
                        nc.scalar.activation(zb[0:n, i, c * BW:(c + 1) * BW], bank[q % 6][0:n, :],
                                             ACT.Copy).then_inc(S("zb_sb"), 1)
                act.wait_ge(S("fx_ready"), 1)
                ch(nc.scalar.activation(lft[:, 1], lft[:, 0], ACT.Abs))
                ch(nc.scalar.activation(lft[:, 2], lft[:, 1], ACT.Exp, scale=-1.0))
                nc.scalar.activation(lft[:, 3], lft[:, 2], ACT.Ln, bias=1.0).then_inc(S("ln1p_ready"), 1)
                act.wait_ge(S("zb_sb"), 9)
                act.wait_ge(S("xT_ps"), 6)
                act.wait_ge(S("xn_used"), 1)
                for i, n in enumerate(ROWS):
                    nc.scalar.activation(sq[0:n, i, :], zb[0:n, i, 0:2 * BW], ACT.Square)\
                        .then_inc(S("qk_sq"), 1)
                act.wait_ge(S("qk_ms"), 1)
                nc.scalar.activation(s16[2], s16[1], ACT.Sqrt).then_inc(S("qk_rt"), 1)
                for j in range(1, ATILES, 2):
                    act.wait_ge(S("za_ps"), j + 1)
                    b = bank[j % 4]
                    nc.scalar.activation(za[:, j, 1:1 + LP], b[:, 0:LP], ACT.Copy)
                    nc.scalar.activation(za[:, j, 1 + LP:ZC].rearrange("p (b c) -> p b c", b=DB)[:, :, 1:],
                                         b[:, LP:T].rearrange("p (b c) -> p b c", b=DB), ACT.Copy)\
                        .then_inc(S("za_sb_odd"), 1)
                for i, n in enumerate(ROWS):
                    act.wait_ge(S("qkT_ps"), 2 * i + 2)
                    nc.scalar.activation(qkT[:, 4:8, i * P:i * P + n],
                                         bank[4 + (2 * i + 1) % 3][:, :].rearrange("p (k t) -> p k t", k=4)[:, :, 0:n],
                                         ACT.Copy).then_inc(S("qkT_b"), 1)

            @block.tensor
            def _(pe):
                ring = Ring()
                pe.wait_ge(S("ident_ready"), 1)
                for i, n in enumerate(ROWS):
                    pe.wait_ge(S("xn_ready"), i + 1)
                    for half in range(2):
                        for k in range(4):
                            kk = 4 * half + k
                            mm = nc.tensor.transpose(bank[2 * i + half][:, k * P:k * P + n],
                                                     xn[0:n, i, kk * P:(kk + 1) * P], ident[0:n, 0:n])
                        mm.then_inc(S("xT_ps"), 1)
                pe.wait_ge(S("prm_in"), 16)
                nc.tensor.transpose(bank[6][:, 0:NPRM], prm_rows[0:NPRM, :], ident[0:NPRM, 0:NPRM])\
                    .then_inc(S("prm_ps"), 1)
                pe.wait_ge(S("shift_in"), 16)
                for j in range(ATILES):
                    mm = nc.tensor.transpose(bank[7][:, j * DB:(j + 1) * DB], shift_tm[:, j * P:(j + 1) * P],
                                             ident[0:DB, 0:DB])
                mm.then_inc(S("shiftT_ps"), 1)
                pe.wait_ge(S("xnT_a"), 3)
                pe.wait_ge(S("xnT_b"), 3)
                for c, pair in enumerate(zslots):
                    for s in pair:
                        ring.fills[s] += 1
                        pe.wait_ge(full[s], 16 * ring.fills[s])
                    for i, n in enumerate(ROWS):
                        q = 3 * c + i
                        if q >= 6:
                            pe.wait_ge(S("zb_sb"), q - 5)
                        for k in range(KT):
                            w = slot[pair[k // 4]].rearrange("p (k n) -> p k n", k=4)
                            mm = nc.tensor.matmul(bank[q % 6][0:n, :], xnT[:, k, i * P:i * P + n], w[:, k % 4, :],
                                                  start=(k == 0), stop=(k == KT - 1))
                        mm.then_inc(S("zb_ps"), 1)
                pe.wait_ge(S("wf_in"), 16)
                pe.wait_ge(S("prm_sb"), 1)
                for i, n in enumerate(ROWS):
                    for k in range(KT):
                        mm = nc.tensor.matmul(bank[6][0:n, i * NH:(i + 1) * NH], xnT[:, k, i * P:i * P + n],
                                              wf[:, k, :], start=(k == 0), stop=(k == KT - 1))
                mm.then_inc(S("f_ps"), 1)
                pe.wait_ge(S("zb_sb"), 9)
                for c, s in enumerate(aslots):
                    ring.fills[s] += 1
                    pe.wait_ge(full[s], 16 * ring.fills[s])
                    w = slot[s].rearrange("p (k n) -> p k n", k=KT)
                    for t in range(2):
                        j = 2 * c + t
                        if j >= 4:
                            pe.wait_ge(S("za_sb_odd" if j % 2 else "za_sb_even"), j // 2 - 1)
                        for k in range(KT):
                            mm = nc.tensor.matmul(bank[j % 4][:, 0:T], w[:, k, t * P:(t + 1) * P], xnT[:, k, :],
                                                  start=(k == 0), stop=(k == KT - 1))
                        mm.then_inc(S("za_ps"), 1)
                pe.wait_ge(S("lf_ready"), 1)
                pe.wait_ge(S("masks_ready"), 1)
                pe.wait_ge(S("shift_sb"), 1)
                for i, n in enumerate((P, P, NMETA)):
                    mm = nc.tensor.matmul(bank[7][0:NH, 0:LP], lf[0:n, i, :], causal01[0:n, i, :],
                                          start=(i == 0), stop=(i == 2))
                mm.then_inc(S("c_ps"), 1)
                nc.tensor.matmul(bank[6][0:ROWS[2], 64:64 + NH], m_si[0:ROWS[2], 2, 0:ROWS[2]], lf[0:ROWS[2], 2, :],
                                 start=True, stop=True).then_inc(S("c_ps"), 1)
                pe.wait_ge(S("qk_ready"), 1)
                pe.wait_ge(S("c_sb"), 2)
                for i, n in enumerate(ROWS):
                    for half in range(2):
                        q = 2 * i + half
                        if q >= 3:
                            pe.wait_ge(S("qkT_a" if (q - 3) % 2 == 0 else "qkT_b"), (q - 3) // 2 + 1)
                        for k in range(4):
                            kk = 4 * half + k
                            mm = nc.tensor.transpose(bank[4 + q % 3][:, k * P:k * P + n],
                                                     zb[0:n, i, kk * P:(kk + 1) * P], ident[0:n, 0:n])
                        mm.then_inc(S("qkT_ps"), 1)
                pe.wait_ge(S("za_sb_even"), 7)
                pe.wait_ge(S("za_sb_odd"), 7)
                for j in range(ATILES):
                    cols = za[:, j, LP:ZC:1 + DS]
                    b = bank[j // 4]
                    mm = nc.tensor.transpose(b[0:1 + DB, (j % 4) * P:(j % 4 + 1) * P], cols, ident)
                mm.then_inc(S("shift_ps"), 1)

            @block.vector
            def _(dve):
                ch = Chain(dve, S("dve_self"))
                ch(nc.vector.memset(ss, 1.0))
                ch(nc.vector.memset(s16[0], 1.0))
                ch(nc.vector.memset(lft[:, 0], 0.0))
                dve.sem_inc(S("stats_zeroed"), 1)
                dve.wait_ge(S("ss_ready"), 3)
                nc.vector.tensor_scalar(ms, ss, 1.0 / DM, RMS_EPS, mult, add).then_inc(S("ms_ready"), 1)
                dve.wait_ge(S("rt_ready"), 1)
                ch(nc.vector.reciprocal(rstd, rt))
                dve.wait_ge(S("ln_in"), 16)
                for i, n in enumerate(ROWS):
                    nc.vector.scalar_tensor_tensor(out=xn[0:n, i, :], in0=xt[0:n, i, :], scalar=rstd[0:n, i:i + 1],
                                                   in1=lnb[0:n, :], op0=mult, op1=mult).then_inc(S("xn_ready"), 1)
                dve.wait_ge(S("xn_ready"), 3)
                dve.sem_inc(S("xn_used"), 1)
                for i, n in enumerate(ROWS):
                    dve.wait_ge(S("xT_ps"), 2 * i + 1)
                    nc.vector.tensor_copy(xnT[:, 0:4, i * P:i * P + n],
                                          bank[2 * i][:, :].rearrange("p (k t) -> p k t", k=4)[:, :, 0:n])\
                        .then_inc(S("xnT_a"), 1)
                dve.wait_ge(S("prm_ps"), 1)
                nc.vector.tensor_copy(prm, bank[6][:, 0:NPRM]).then_inc(S("prm_sb"), 1)
                dve.wait_ge(S("shiftT_ps"), 1)
                nc.vector.tensor_copy(za[:, :, 1 + LP:ZC:1 + DS],
                                      bank[7][:, 0:ATILES * DB].rearrange("p (j b) -> p j b", b=DB))\
                    .then_inc(S("shift_sb"), 1)
                dve.wait_ge(S("f_ps"), 1)
                dve.wait_ge(S("fp_in"), 32)
                for i, n in enumerate(ROWS):
                    ch(nc.vector.tensor_tensor(lft[0:n, 0, i, :], bank[6][0:n, i * NH:(i + 1) * NH], fb[0:n, :], add))
                dve.sem_inc(S("fx_ready"), 1)
                dve.wait_ge(S("ln1p_ready"), 1)
                nc.vector.scalar_tensor_tensor(out=lf, in0=lft[:, 0], scalar=0.0, in1=lft[:, 3], op0=vmin, op1=sub)\
                    .then_inc(S("lf_ready"), 1)
                dve.wait_ge(S("qk_sq"), 3)
                for i, n in enumerate(ROWS):
                    ch(nc.vector.tensor_reduce(s16[0][0:n, i, :], sq[0:n, i, :].rearrange("p (h d) -> p h d", d=HD),
                                               AX.X, add))
                nc.vector.tensor_scalar(s16[1], s16[0], 1.0 / HD, RMS_EPS, mult, add).then_inc(S("qk_ms"), 1)
                dve.wait_ge(S("qk_rt"), 1)
                ch(nc.vector.reciprocal(s16[3], s16[2]))
                ch(nc.vector.tensor_scalar(s16[3][:, :, 0:NH], s16[3][:, :, 0:NH], HD ** -0.5, None, mult))

                def za_out(j):
                    dve.wait_ge(S("za_ps"), j + 1)
                    b = bank[j % 4]
                    nc.vector.tensor_copy(za[:, j, 1:1 + LP], b[:, 0:LP])
                    nc.vector.tensor_copy(za[:, j, 1 + LP:ZC].rearrange("p (b c) -> p b c", b=DB)[:, :, 1:],
                                          b[:, LP:T].rearrange("p (b c) -> p b c", b=DB))\
                        .then_inc(S("za_sb_even"), 1)

                for i, n in enumerate(ROWS):
                    z = zb[0:n, i, 0:2 * BW].rearrange("p (h d) -> p h d", d=HD)
                    ch(nc.vector.tensor_tensor(z, z, bc(s16[3][0:n, i, :], 2, HD), mult))
                    z = zb[0:n, i, 0:2 * BW].rearrange("p (g h d) -> p g h d", g=2, d=HD)
                    ch(nc.vector.tensor_tensor(z, z, bc(qkn[0:n], 2, NH), mult))
                    za_out(2 * i)
                dve.sem_inc(S("qk_ready"), 1)
                for j in range(6, ATILES, 2):
                    za_out(j)
                dve.wait_ge(S("c_ps"), 2)
                nc.vector.tensor_copy(cT, bank[7][0:NH, 0:LP]).then_inc(S("c_sb"), 1)
                nc.vector.tensor_copy(cn_tm[0:ROWS[2], :], bank[6][0:ROWS[2], 64:64 + NH]).then_inc(S("c_sb"), 1)
                dve.wait_ge(S("c_sb"), 2)
                dve.sem_inc(S("cn_ready"), 1)
                for i, n in enumerate(ROWS):
                    dve.wait_ge(S("qkT_ps"), 2 * i + 1)
                    nc.vector.tensor_copy(qkT[:, 0:4, i * P:i * P + n],
                                          bank[4 + (2 * i) % 3][:, :].rearrange("p (k t) -> p k t", k=4)[:, :, 0:n])\
                        .then_inc(S("qkT_a"), 1)
                dve.wait_ge(S("qkT_a"), 3)
                dve.wait_ge(S("qkT_b"), 3)
                dve.wait_ge(S("masks_ready"), 1)
                for e in range(2):
                    src = qkT[e * HD:(e + 1) * HD, 0:4, LP:T].rearrange("p g (b t) -> p b g t", b=DB)
                    ch(nc.vector.tensor_copy(q_all[e * HD:(e + 1) * HD, :, :, e * DS:(e + 1) * DS], src))
                ch(nc.vector.tensor_copy(knT, qkT[:, 4:8, LP:T]))
                dve.wait_ge(S("shift_ps"), 1)
                for q in range(4):
                    w = min(512, AP_ - 512 * q)
                    ch(nc.vector.tensor_copy(shift_out[:, 512 * q:512 * q + w], bank[q][0:1 + DB, 0:w]))
                dve.sem_inc(S("shift_ready"), 1)


        retire()

        sp2 = Space(arena, mark1, NF)
        fq = sp2(2, LP)
        fk = sp2(LP)
        fv = sp2(NT, P)
        fsel = sp2(2, P, parts=NH)
        fs = sp2(6, LP)
        fpt = sp2(6, NT, P)
        fmx, fnm, fsum, frs = (sp2(6) for _ in range(4))
        NQ, NK = [P, P, NMETA], [P, 2 * P, LP]
        cases = [(e, i) for e in range(2) for i in range(NT)]
        C = len(cases)

        with nc.Block("fox") as block:
            @block.sync
            def _(sp):
                pass

            @block.gpsimd
            def _(pool):
                ch = Chain(pool, S("fox_pool"))
                ch(nc.gpsimd.memset(fq, 0.0))
                start, per = ch.n, 6
                with pool.Fori(0, NPAIR) as g:
                    ch.n, ch.at = 0, g * per + start
                    pool.wait_ge(S("fo_ps"), g + 1)
                    for e in range(2):
                        r = slice(e * HD, (e + 1) * HD)
                        ch(nc.gpsimd.tensor_copy(fq[r, e, :], qkT[r, bass.ds(g, 1), 0:LP].rearrange("p a t -> p (a t)")))
                        ch(nc.gpsimd.tensor_copy(fsel[:, e, :], selneg[:, bass.ds(2 * g + e, 1), :]
                                                 .rearrange("p a t -> p (a t)")))
                    ch(nc.gpsimd.tensor_copy(fk, qkT[:, bass.ds(g + NPAIR, 1), 0:LP].rearrange("p a t -> p (a t)")))
                    ch(nc.gpsimd.tensor_copy(fv[:, 0:2, :], zb[:, 0:2, bass.ds(2 * BW + g * P, P)]))
                    assert ch.n == per
                    nc.gpsimd.tensor_copy(fv[0:NMETA, 2, :], zb[0:NMETA, 2, bass.ds(2 * BW + g * P, P)])\
                        .then_inc(S("fox_in"), 1)

            @block.tensor
            def _(pe):
                pe.sem_inc(S("fo_ps"), 1)
                with pe.Fori(0, NPAIR) as g:
                    pe.wait_ge(S("fox_in"), g + 1)
                    pe.wait_ge(S("fo_sb"), g + 1)
                    for m, (e, i) in enumerate(cases):
                        nq, nk = NQ[i], NK[i]
                        nc.tensor.matmul(bank[m][0:nq, 0:nk], fq[:, e, i * P:i * P + nq], fk[:, 0:nk],
                                         start=True, stop=False)
                        nc.tensor.matmul(bank[m][0:nq, 0:nk], fsel[:, e, 0:nq], cT[:, 0:nk],
                                         start=False, stop=True).then_inc(S("fs_ps"), 1)
                    for m, (e, i) in enumerate(cases):
                        nq, nk = NQ[i], NK[i]
                        if i < 2:
                            pe.wait_ge(S("fp_ready"), g * C + m + 1 + i)
                            if m >= 1:
                                pe.wait_ge(S("fpt_sb"), g * C + m)
                        for t in range(i + 1):
                            w = min(P, nk - t * P)
                            mm = nc.tensor.transpose(bank[6 + m % 2][0:w, t * P:t * P + nq],
                                                     fs[0:nq, m, t * P:t * P + w], ident[0:nq, 0:nq])
                        mm.then_inc(S("fpt_ps"), 1)
                    pe.wait_ge(S("fpt_sb"), g * C + C)
                    for m, (e, i) in enumerate(cases):
                        nq, nk = NQ[i], NK[i]
                        for t in range(i + 1):
                            w = min(P, nk - t * P)
                            mm = nc.tensor.matmul(bank[0][e * HD:(e + 1) * HD, i * P:i * P + nq],
                                                  fv[0:w, t, e * HD:(e + 1) * HD], fpt[0:w, m, t, 0:nq],
                                                  start=(t == 0), stop=(t == i))
                    mm.then_inc(S("fo_ps"), 1)

            @block.scalar
            def _(act):
                with act.Fori(0, NPAIR) as g:
                    for m, (e, i) in enumerate(cases):
                        nq, nk = NQ[i], NK[i]
                        act.wait_ge(S("fnm_ready"), g * C + m + 1)
                        nc.scalar.activation(fs[0:nq, m, 0:nk], fs[0:nq, m, 0:nk], ACT.Exp, bias=fnm[0:nq, m:m + 1],
                                             accum_out=fsum[0:nq, m:m + 1]).then_inc(S("fe_ready"), 1)
                    for m, (e, i) in enumerate(cases):
                        nq, nk = NQ[i], NK[i]
                        act.wait_ge(S("fpt_ps"), g * C + m + 1)
                        if i < 2:
                            nc.scalar.activation(fpt[:, m, 0:i + 1, :], bank[6 + m % 2][:, 0:(i + 1) * P]
                                                 .rearrange("p (t q) -> p t q", q=P), ACT.Copy)\
                                .then_inc(S("fpt_sb"), 1)
                        else:
                            nc.scalar.activation(fpt[:, m, 0:2, 0:nq], bank[6 + m % 2][:, 0:2 * P]
                                                 .rearrange("p (t q) -> p t q", q=P)[:, :, 0:nq], ACT.Copy)
                            nc.scalar.activation(fpt[0:NMETA, m, 2, 0:nq], bank[6 + m % 2][0:NMETA, 2 * P:2 * P + nq],
                                                 ACT.Copy).then_inc(S("fpt_sb"), 1)

            @block.vector
            def _(dve):
                ch = Chain(dve, S("fox_dve"))
                dve.sem_inc(S("fo_sb"), 1)
                per = 3 * C
                with dve.Fori(0, NPAIR) as g:
                    ch.n, ch.at = 0, g * per
                    for m, (e, i) in enumerate(cases):
                        nq, nk = NQ[i], NK[i]
                        dve.wait_ge(S("fs_ps"), g * C + m + 1)
                        ch(nc.vector.tensor_tensor(fs[0:nq, m, 0:nk], bank[m][0:nq, 0:nk], addmask[0:nq, i, 0:nk], add))
                        ch(nc.vector.tensor_reduce(fmx[0:nq, m:m + 1], fs[0:nq, m, 0:nk], AX.X, vmax))
                        nc.vector.tensor_scalar(fnm[0:nq, m:m + 1], fmx[0:nq, m:m + 1], -1.0, None, mult)\
                            .then_inc(S("fnm_ready"), 1)
                    for m, (e, i) in enumerate(cases):
                        nq, nk = NQ[i], NK[i]
                        dve.wait_ge(S("fe_ready"), g * C + m + 1)
                        ch(nc.vector.reciprocal(frs[0:nq, m:m + 1], fsum[0:nq, m:m + 1]))
                        nc.vector.tensor_scalar(fs[0:nq, m, 0:nk], fs[0:nq, m, 0:nk], frs[0:nq, m:m + 1], None, mult)\
                            .then_inc(S("fp_ready"), 1)
                    assert ch.n == per
                    dve.wait_ge(S("fo_ps"), g + 2)
                    nc.vector.tensor_copy(obT[:, bass.ds(g, 1), 0:LP].rearrange("p a t -> p (a t)"), bank[0][:, 0:LP])\
                        .then_inc(S("fo_sb"), 1)

        retire()

        sp3 = Space(arena, base + ATILES * ZC, NF)
        low = Space(arena, base, base + ATILES * ZC)
        gate = sp3(NPAIR, T)
        bonus = sp3(NPAIR, T)
        ar = sp3(5, NPAIR, TW)
        pend = sp3(NPAIR, NCH + DB)
        mark3 = sp3.at
        diff = sp3(ATILES, ZC - 1)
        kraw, sg, av, cs = (sp3(NPAIR, T) for _ in range(4))
        kkr = sp3(NPAIR, T)
        z12, z13, thw, sgl = (sp3(T) for _ in range(4))
        lora = sp3(2, AW)
        reset = bonus[:, 0, :]
        f4 = lambda a: a.rearrange("p g t -> p (g t)")
        dv = diff.rearrange("p j t -> p (j t)")
        tmp, pex, pin = (dv[:, i * NPAIR * T:(i + 1) * NPAIR * T].rearrange("p (g t) -> p g t", g=NPAIR)
                         for i in range(3))
        AL, BE, KA_, RH, VV = range(5)
        arT = lambda i: ar[:, i, :, 0:T]

        def split(ap):
            return ap[:, 0:LP], ap[:, LP:T].rearrange("p (b t) -> p b t", b=DB)

        with nc.Block("rwkv_pre") as block:
            @block.sync
            def _(sp):
                sp.dma_start(lora, A["lora"]).then_inc(S("lora_in"), 16)

            @block.gpsimd
            def _(pool):
                ch = Chain(pool, S("pre_pool"))
                nc.gpsimd.memset(ar, 0.0).then_inc(S("ar_zero"), 1)
                ch(nc.gpsimd.memset(reset, 1.0))
                ch(nc.gpsimd.memset(reset[:, 0:LP:CH], 0.0))
                ch(nc.gpsimd.memset(reset[:, LP:T:DS], 0.0))
                pool.sem_inc(S("reset_ready"), 1)

            @block.tensor
            def _(pe):
                pe.wait_ge(S("lora_in"), 16)
                pe.wait_ge(S("th_ready"), 1)
                for g in range(NPAIR):
                    nc.tensor.matmul(bank[g][:, 0:T], lora[0:LORA, 0, g * P:(g + 1) * P], thw[0:LORA, :],
                                     start=True, stop=True).then_inc(S("w_ps"), 1)
                for g in range(NPAIR):
                    nc.tensor.matmul(bank[4 + g][:, 0:T], lora[LORA:P, 0, g * P:(g + 1) * P], z12[LORA:P, :],
                                     start=True, stop=True).then_inc(S("a_ps"), 1)
                pe.wait_ge(S("sgl_ready"), 1)
                pe.wait_ge(S("sg_sb"), 4)
                for g in range(NPAIR):
                    nc.tensor.matmul(bank[g][:, 0:T], lora[:, 1, g * P:(g + 1) * P], sgl,
                                     start=True, stop=True).then_inc(S("g_ps"), 1)
                pe.wait_ge(S("a_sb"), 4)
                pe.wait_ge(S("kk_sq"), 1)
                for g in range(NPAIR):
                    nc.tensor.matmul(bank[4 + g][:, 0:T], headones, tmp[:, g, :], start=True, stop=True)\
                        .then_inc(S("kn_ps"), 1)
                pe.wait_ge(S("rkk_ready"), 1)
                pe.wait_ge(S("gate_sb"), 4)
                for g in range(NPAIR):
                    nc.tensor.matmul(bank[g][:, 0:T], headones, pex[:, g, :], start=True, stop=True)\
                        .then_inc(S("bon_ps"), 1)

            @block.scalar
            def _(act):
                act.wait_ge(S("z12_ready"), 2)
                nc.scalar.activation(thw[0:LORA, :], z12[0:LORA, :], ACT.Tanh).then_inc(S("th_ready"), 1)
                nc.scalar.activation(sgl, z13, ACT.Sigmoid).then_inc(S("sgl_ready"), 1)
                for g in range(NPAIR):
                    act.wait_ge(S("w_ps"), g + 1)
                    nc.scalar.activation(sg[:, g, :], bank[g][:, 0:T], ACT.Sigmoid, bias=prm[:, W0 + g:W0 + g + 1])\
                        .then_inc(S("sg_sb"), 1)
                for g in range(NPAIR):
                    act.wait_ge(S("a_ps"), g + 1)
                    nc.scalar.activation(av[:, g, :], bank[4 + g][:, 0:T], ACT.Sigmoid,
                                         bias=prm[:, A0 + g:A0 + g + 1]).then_inc(S("a_sb"), 1)
                act.wait_ge(S("kkr_ready"), 1)
                nc.scalar.activation(tmp, kkr, ACT.Square).then_inc(S("kk_sq"), 1)
                for g in range(NPAIR):
                    act.wait_ge(S("g_ps"), g + 1)
                    nc.scalar.activation(gate[:, g, :], bank[g][:, 0:T], ACT.Copy).then_inc(S("gate_sb"), 1)
                act.wait_ge(S("kn_ready"), 1)
                nc.scalar.activation(tmp, tmp, ACT.Sqrt).then_inc(S("kn_rt"), 1)
                act.wait_ge(S("cs_ready"), 1)
                act.wait_ge(S("bonus_ready"), 1)
                nc.scalar.activation(pin, cs, ACT.Exp, scale=DECAY).then_inc(S("pin_ready"), 1)
                nc.scalar.activation(pex, sg, ACT.Exp, scale=-DECAY).then_inc(S("pex_ready"), 1)
                nc.scalar.activation(cs, cs, ACT.Exp, scale=-DECAY).then_inc(S("p_ready"), 1)

            @block.vector
            def _(dve):
                ch = Chain(dve, S("pre_dve"))
                ch(nc.vector.tensor_tensor(diff, za[:, :, 0:ZC - 1], za[:, :, 1:ZC], sub))

                def shifted(j, out):
                    op, os_ = split(out)
                    mu = prm[:, MU + j:MU + j + 1]
                    nc.vector.scalar_tensor_tensor(out=op, in0=diff[:, j, 0:LP], scalar=mu, in1=za[:, j, 1:1 + LP],
                                                   op0=mult, op1=add)
                    return nc.vector.scalar_tensor_tensor(
                        out=os_, in0=diff[:, j, LP:ZC - 1].rearrange("p (b t) -> p b t", t=DS + 1)[:, :, 1:], scalar=mu,
                        in1=za[:, j, 1 + LP:ZC].rearrange("p (b t) -> p b t", t=DS + 1)[:, :, 1:], op0=mult, op1=add)

                shifted(12, z12).then_inc(S("z12_ready"), 1)
                shifted(13, z13).then_inc(S("z12_ready"), 1)
                for g in range(NPAIR):
                    ch(shifted(4 + g, kraw[:, g, :]))
                for g in range(NPAIR):
                    ch(nc.vector.tensor_scalar(kkr[:, g, :], kraw[:, g, :], prm[:, KK + g:KK + g + 1], None, mult))
                dve.wait_ge(S("ar_zero"), 1)
                for g in range(NPAIR):
                    ch(shifted(g, ar[:, RH, g, 0:T]))
                    ch(shifted(8 + g, ar[:, VV, g, 0:T]))
                dve.sem_inc(S("kkr_ready"), 1)
                dve.wait_ge(S("reset_ready"), 1)
                dve.wait_ge(S("sg_sb"), 4)
                for g in range(NPAIR):
                    ch(nc.vector.tensor_tensor_scan(cs[:, g, :], reset, sg[:, g, :], 0.0, mult, add))
                ch(nc.vector.tensor_tensor(sg, cs, sg, sub))
                dve.sem_inc(S("cs_ready"), 1)
                dve.wait_ge(S("a_sb"), 4)
                for g in range(NPAIR):
                    ch(nc.vector.tensor_scalar(pin[:, g, :], av[:, g, :], 1.0, prm[:, KA + g:KA + g + 1], sub, mult))
                ch(nc.vector.scalar_tensor_tensor(out=f4(kraw), in0=f4(pin), scalar=1.0, in1=f4(kraw),
                                                  op0=add, op1=mult))
                for g in range(NPAIR):
                    ch(nc.vector.scalar_tensor_tensor(out=pex[:, g, :], in0=ar[:, RH, g, 0:T],
                                                      scalar=prm[:, RK + g:RK + g + 1], in1=kraw[:, g, :],
                                                      op0=mult, op1=mult))
                dve.sem_inc(S("rkk_ready"), 1)
                dve.wait_ge(S("kn_ps"), 4)
                for g in range(NPAIR):
                    ch(nc.vector.tensor_scalar(tmp[:, g, :], bank[4 + g][:, 0:T], 1e-24, None, vmax))
                dve.sem_inc(S("kn_ready"), 1)
                for g in range(NPAIR):
                    dve.wait_ge(S("bon_ps"), g + 1)
                    ch(nc.vector.tensor_tensor(bonus[:, g, :], bank[g][:, 0:T], ar[:, VV, g, 0:T], mult))
                dve.sem_inc(S("bonus_ready"), 1)
                dve.wait_ge(S("kn_rt"), 1)
                ch(nc.vector.reciprocal(f4(tmp), f4(tmp)))
                ch(nc.vector.tensor_tensor(kkr, kkr, tmp, mult))
                ch(nc.vector.tensor_tensor(av, av, kkr, mult))
                dve.wait_ge(S("pin_ready"), 1)
                ch(nc.vector.tensor_tensor(arT(BE), av, pin, mult))
                ch(nc.vector.tensor_tensor(arT(KA_), kraw, pin, mult))
                dve.wait_ge(S("pex_ready"), 1)
                ch(nc.vector.tensor_tensor(arT(AL), kkr, pex, mult))
                dve.wait_ge(S("p_ready"), 1)
                ch(nc.vector.tensor_tensor(arT(RH), arT(RH), cs, mult))
                ch(nc.vector.tensor_copy(pend[:, :, 0:NCH], cs[:, :, CH - 1:LP:CH]))
                ch(nc.vector.tensor_copy(pend[:, :, NCH:], cs[:, :, LP + DS - 1:T:DS]))

        retire()

        assert low.at == base
        mats = low(4, 2, NT, P)
        half = 2 * 2 * NT * P
        sout = arena[0:HD, base + half:base + half + (1 + DB) * P].rearrange("p (i t) -> p i t", t=P)
        snew = low(1 + DB, HD)
        x1t, x1, x2t, x2 = (mats[:, i] for i in range(4))
        us = low(DB, P)
        sp4 = Space(arena, mark3, NF)
        pr5 = sp4(5, TW)
        bek, kek = sp4(TW), sp4(TW)
        betm, ketm, vtm = (sp4(NT, P) for _ in range(3))
        rr = sp4(NT, 2, 2, HD)
        bt, ct, dt_ = (sp4(2, NT, P) for _ in range(3))
        vm2, xm2, um2 = (sp4(NT, 2, P) for _ in range(3))
        uu, wt = sp4(NT, P), sp4(NT, P)
        sbd = sp4(2, P)
        s0bd = sp4(DB, P)
        stin = sp4(DB, P, parts=HD)
        vm8 = sp4(DB, P)
        ppend = sp4(NCH + DB)
        otmp, ut = sp4(T), sp4(P)
        assert CH == 16 and NCH == 17 and LP - 2 * P == CH

        def half_mask(s):
            return bc(cm2[:, s:s + 1], 2, P).broadcast_to([P, NT, P])

        def b3(b):
            return bank[b][:, 0:NT * P].rearrange("p (j t) -> p j t", j=NT)

        with nc.Block("rwkv_pairs") as block:
            @block.sync
            def _(sp):
                sview = A["state"].rearrange("b (g h) v k -> g b v h k", h=2)
                sp.sem_inc(S("rw_free"), 1)
                with sp.Fori(0, NPAIR) as g:
                    sp.wait_ge(S("st_ps"), g + 1)
                    for b in range(DB):
                        sp.dma_start(stin[:, b, :].rearrange("p (h k) -> p h k", h=2),
                                     sview[bass.ds(g, 1), b].rearrange("a v h k -> (a v) h k")).then_inc(S("st_in"), 16)
                    sp.wait_ge(S("so_sb"), g * 3 + 3)
                    rp = O["rw_p"].rearrange("(g h) v k -> g v h k", h=2)
                    rs_ = O["rw_s"].rearrange("b (g h) v k -> g b v h k", h=2)
                    sp.dma_start(rp[bass.ds(g, 1)].rearrange("a v h k -> (a v) h k"),
                                 sout[:, 0, :].rearrange("p (h k) -> p h k", h=2)).then_inc(S("rw_out"), 16)
                    for b in range(DB):
                        sp.dma_start(rs_[bass.ds(g, 1), b].rearrange("a v h k -> (a v) h k"),
                                     sout[:, 1 + b, :].rearrange("p (h k) -> p h k", h=2)).then_inc(S("rw_out"), 16)
                    sp.wait_ge(S("rw_out"), (g + 1) * ((1 + DB) * 16))
                    sp.sem_inc(S("rw_free"), 1)

            @block.gpsimd
            def _(pool):
                ch = Chain(pool, S("pair_pool"))
                for m in (um2, bek, kek, s0bd, sbd):
                    ch(nc.gpsimd.memset(m, 0.0))
                start, per = ch.n, 15
                with pool.Fori(0, NPAIR) as g:
                    ch.n, ch.at = 0, g * per + start
                    pool.wait_ge(S("pair_done"), g + 1)
                    ch(nc.gpsimd.tensor_copy(pr5, ar[:, :, bass.ds(g, 1), :].rearrange("p i a t -> p (i a) t")))
                    pool.sem_inc(S("pr5_ready"), 1)
                    ch(nc.gpsimd.tensor_copy(ppend, pend[:, bass.ds(g, 1), :].rearrange("p a t -> p (a t)")))
                    for src, dst in ((BE, bek), (KA_, kek)):
                        for lo, hi, n, w in ((0, LP, NCH, CH), (LP, T, DB, DS)):
                            v = lambda a: a[:, lo:hi].rearrange("p (c t) -> p c t", t=w)
                            o = 0 if lo == 0 else NCH
                            ch(nc.gpsimd.tensor_tensor(v(dst), v(pr5[:, src, :]), bc(ppend[:, o:o + n], 2, w), mult))
                    pool.sem_inc(S("bek_ready"), 1)
                    ch(nc.gpsimd.memset(sbd[:, 0, :], 0.0))
                    pool.sem_inc(S("s_zero"), 1)
                    pool.wait_ge(S("vtm_sb"), g + 1)
                    for s in range(2):
                        ch(nc.gpsimd.tensor_tensor(vm2[:, :, s, :], vtm, half_mask(s), mult))
                    pool.sem_inc(S("vm2_ready"), 1)
                    ch(nc.gpsimd.tensor_tensor(vm8, bc(vtm[:, 2, :], 1, DB), bc(cm8, 2, P), mult))
                    pool.sem_inc(S("vm8_ready"), 1)
                    pool.wait_ge(S("r_ready"), g * 2 + 2)
                    for s in range(2):
                        ch(nc.gpsimd.tensor_tensor(xm2[:, :, s, :], rr[:, :, 1].rearrange("p j h v -> p j (h v)"),
                                                   half_mask(s), mult))
                    pool.sem_inc(S("xm2_ready"), 1)
                    for q in range(2):
                        pool.wait_ge(S("us_raw"), g * 2 + q + 1)
                        v = us[:, 4 * q:4 * q + 4, :]
                        ch(nc.gpsimd.tensor_tensor(v, v, bc(cm8[:, 4 * q:4 * q + 4], 2, P), mult))
                        pool.sem_inc(S("us_ready"), 1)
                    pool.wait_ge(S("um_ready"), g * NCH + NCH)
                    ch(nc.gpsimd.tensor_tensor(uu, um2[:, :, 0, :], um2[:, :, 1, :], add))
                    pool.sem_inc(S("uu_raw"), 1)
                    assert ch.n == per, ch.n

            @block.tensor
            def _(pe):
                pe.sem_inc(S("st_ps"), 1)
                hs = [slice(h * HD, (h + 1) * HD) for h in range(2)]

                def products(out, lhs, rhs, name):
                    for h in range(2):
                        for j in range(NT):
                            mm = nc.tensor.matmul(bank[out[h]][:, j * P:(j + 1) * P], lhs(h, j), rhs(h, j),
                                                  start=True, stop=True)
                        mm.then_inc(S(name), 1)

                def fm(i):
                    return lambda h, j: pr5[hs[h], i, j * P:(j + 1) * P]

                def tm(m):
                    return lambda h, j: m[:, h, j, :]

                rh = lambda h, j: rr[:, j, :, h, :]
                with pe.Fori(0, NPAIR) as g:
                    pe.wait_ge(S("pr5_ready"), g + 1)
                    for i, b, name in ((AL, 0, "alT_ps"), (VV, 1, "vT_ps")):
                        for j in range(NT):
                            mm = nc.tensor.transpose(bank[b][:, j * P:(j + 1) * P], pr5[:, i, j * P:(j + 1) * P], ident)
                        mm.then_inc(S(name), 1)
                    products((2, 3), fm(BE), fm(AL), "at_ps")
                    products((4, 5), fm(KA_), fm(AL), "bt_ps")
                    products((6, 7), fm(AL), fm(BE), "a_m_ps")
                    pe.wait_ge(S("bek_ready"), g + 1)
                    pe.wait_ge(S("al_sb"), g + 1)
                    pe.wait_ge(S("vtm_sb"), g + 1)
                    for src, b, name in ((bek, 0, "beT_ps"), (kek, 1, "keT_ps")):
                        for j in range(NT):
                            mm = nc.tensor.transpose(bank[b][:, j * P:(j + 1) * P], src[:, j * P:(j + 1) * P], ident)
                        mm.then_inc(S(name), 1)
                    pe.wait_ge(S("at_sb"), g * 2 + 2)
                    pe.wait_ge(S("bt_sb"), g * 2 + 2)
                    for h in range(2):
                        for j in range(NT):
                            mm = nc.tensor.matmul(bank[2][:, (2 * j + h) * HD:(2 * j + h + 1) * HD], bt[:, h, j, :],
                                                  vtm[:, j, hs[h]], start=True, stop=True)
                    mm.then_inc(S("bv_ps"), 1)
                    pe.wait_ge(S("a_m_sb"), g * 2 + 2)
                    products((6, 7), tm(x1), tm(x1t), "sqt_ps")
                    pe.wait_ge(S("betm_sb"), g * 2 + 2)
                    products((0, 1), tm(x1t), tm(x1), "sq_ps")
                    pe.wait_ge(S("bv_sb"), g + 1)
                    products((4, 5), tm(x1t), rh, "ap_ps")
                    products((2, 3), fm(BE), fm(RH), "ct_ps")
                    pe.wait_ge(S("sqt_sb"), g * 6 + 2)
                    pe.wait_ge(S("sq_sb"), g * 4 + 2)
                    products((6, 7), tm(x2), tm(x2t), "sqt_ps")
                    products((0, 1), tm(x2t), tm(x2), "sq_ps")
                    pe.wait_ge(S("r_step"), g * 8 + 2)
                    products((4, 5), tm(x2t), rh, "ap_ps")
                    pe.wait_ge(S("ct_sb"), g * 2 + 2)
                    products((2, 3), fm(KA_), fm(RH), "dt_ps")
                    pe.wait_ge(S("sqt_sb"), g * 6 + 4)
                    pe.wait_ge(S("sq_sb"), g * 4 + 4)
                    products((6, 7), tm(x1), tm(x1t), "sqt_ps")
                    pe.wait_ge(S("st_in"), (g + 1) * (16 * DB))
                    pe.wait_ge(S("r_step"), g * 8 + 4)
                    products((4, 5), tm(x1t), rh, "ap_ps")
                    for b in range(DB):
                        mm = nc.tensor.transpose(bank[0][:, b * HD:(b + 1) * HD], stin[:, b, :], ident[0:HD, 0:HD])
                    mm.then_inc(S("st_ps"), 1)
                    pe.wait_ge(S("sqt_sb"), g * 6 + 6)
                    pe.wait_ge(S("r_step"), g * 8 + 6)
                    products((4, 5), tm(x2t), rh, "ap_ps")
                    pe.wait_ge(S("r_ready"), g * 2 + 2)
                    for j in range(NT):
                        mm = nc.tensor.transpose(bank[1][:, j * P:(j + 1) * P],
                                                 rr[:, j, 0].rearrange("p h k -> p (h k)"), ident)
                    mm.then_inc(S("wt_ps"), 1)
                    pe.wait_ge(S("wt_sb"), g + 1)
                    pe.wait_ge(S("s0_sb"), g * 2 + 2)
                    pe.wait_ge(S("dt_sb"), g * 2 + 2)
                    for q in range(2):
                        nc.tensor.matmul(bank[6 + q][:, :], wt[:, 2, :],
                                         s0bd[:, 4 * q:4 * q + 4, :].rearrange("p b v -> p (b v)"),
                                         start=True, stop=True).then_inc(S("us_ps"), 1)
                    for b in range(DB):
                        mm = nc.tensor.matmul(bank[4][:, LP + b * DS:LP + (b + 1) * DS], s0bd[:, b, :],
                                              pr5[:, RH, LP + b * DS:LP + (b + 1) * DS], start=True, stop=True)
                    pe.wait_ge(S("vm2_ready"), g + 1)
                    pe.wait_ge(S("s_zero"), g + 1)

                    def chain_step(c):
                        j, r, s = c // 8, slice(32 * (c % 8 // 2), 32 * (c % 8 // 2) + 32), c % 2
                        if c:
                            pe.wait_ge(S("s_ready"), g * NCH + c)
                        nc.tensor.matmul(bank[c % 2][r, 0:P], wt[:, j, r], sbd[:, c % 2, :], start=True, stop=True)\
                            .then_inc(S("u_ps"), 1)
                        mm = nc.tensor.matmul(bank[4][:, c * CH:(c + 1) * CH], sbd[:, c % 2, :],
                                              pr5[:, RH, c * CH:(c + 1) * CH], start=True, stop=True)
                        if c == NCH - 1:
                            mm.then_inc(S("ox_ps"), 1)
                        nc.tensor.matmul(bank[2 + c % 2][:, 0:P], ketm[r, j, :], vm2[r, j, s, :],
                                         start=True, stop=False)
                        pe.wait_ge(S("um_ready"), g * NCH + c + 1)
                        nc.tensor.matmul(bank[2 + c % 2][:, 0:P], betm[r, j, :], um2[r, j, s, :],
                                         start=False, stop=True).then_inc(S("s_ps"), 1)

                    for c in range(NCH):
                        chain_step(c)
                        if c in (4, 6):
                            q = (c - 4) // 2
                            if q == 0:
                                pe.wait_ge(S("vm8_ready"), g + 1)
                            pe.wait_ge(S("us_ready"), g * 2 + q + 1)
                            nc.tensor.matmul(bank[6 + q][:, :], ketm[:, 2, :],
                                             vm8[:, 4 * q:4 * q + 4, :].rearrange("p b v -> p (b v)"),
                                             start=True, stop=False)
                            nc.tensor.matmul(bank[6 + q][:, :], betm[:, 2, :],
                                             us[:, 4 * q:4 * q + 4, :].rearrange("p b v -> p (b v)"),
                                             start=False, stop=True).then_inc(S("sn_ps"), 1)
                    pe.wait_ge(S("uu_ready"), g + 1)
                    pe.wait_ge(S("s_ready"), g * NCH + NCH)
                    for j in range(NT):
                        for h in range(2):
                            nc.tensor.matmul(bank[j][hs[h], 0:P], vtm[:, j, hs[h]], dt_[:, h, j, :],
                                             start=True, stop=False)
                            if (j, h) == (NT - 1, 1):
                                pe.wait_ge(S("snew_ready"), g + 1)
                            mm = nc.tensor.matmul(bank[j][hs[h], 0:P], uu[:, j, hs[h]], ct[:, h, j, :],
                                                  start=False, stop=True)
                    mm.then_inc(S("ocd_ps"), 1)
                    for i in range(1 + DB):
                        mm = nc.tensor.transpose(bank[5 + i // 4][0:HD, (i % 4) * P:(i % 4 + 1) * P],
                                                 snew[:, i, :], ident)
                        if i in (3, 7, 8):
                            mm.then_inc(S("so_ps"), 1)

            @block.scalar
            def _(act):
                with act.Fori(0, NPAIR) as g:
                    act.wait_ge(S("alT_ps"), g + 1)
                    nc.scalar.activation(rr[:, :, 0].rearrange("p j h k -> p j (h k)"), b3(0), ACT.Copy, scale=-1.0)\
                        .then_inc(S("al_sb"), 1)
                    act.wait_ge(S("vT_ps"), g + 1)
                    nc.scalar.activation(vtm, b3(1), ACT.Copy).then_inc(S("vtm_sb"), 1)
                    act.wait_ge(S("beT_ps"), g + 1)
                    nc.scalar.activation(betm, b3(0), ACT.Copy).then_inc(S("betm_sb"), 1)
                    act.wait_ge(S("keT_ps"), g + 1)
                    nc.scalar.activation(ketm, b3(1), ACT.Copy).then_inc(S("betm_sb"), 1)
                    act.wait_ge(S("bv_ps"), g + 1)
                    nc.scalar.activation(rr[:, :, 1], bank[2][:, 0:NT * P].rearrange("p (j h v) -> p j h v", j=NT, h=2),
                                         ACT.Copy, scale=-1.0).then_inc(S("bv_sb"), 1)
                    act.wait_ge(S("rw_free"), g + 1)
                    for n, (mt, m) in enumerate(((x2t, x2), (x1t, x1), (x2t, None))):
                        for h in range(2):
                            act.wait_ge(S("sqt_ps"), g * 6 + 2 * n + h + 1)
                            if h == 0:
                                act.wait_ge(S("ap_ps"), g * 8 + 2 * n) if n else None
                            nc.scalar.activation(mt[:, h], b3(6 + h), ACT.Copy).then_inc(S("sqt_sb"), 1)
                        if m is not None:
                            for h in range(2):
                                act.wait_ge(S("sq_ps"), g * 4 + 2 * n + h + 1)
                                nc.scalar.activation(m[:, h], b3(h), ACT.Copy).then_inc(S("sq_sb"), 1)
                    act.wait_ge(S("st_ps"), g + 2)
                    for h in range(2):
                        r = slice(h * HD, (h + 1) * HD)
                        nc.scalar.activation(s0bd[r, :, r], bank[0][r, :].rearrange("p (b v) -> p b v", b=DB), ACT.Copy)\
                            .then_inc(S("s0_sb"), 1)
                    act.wait_ge(S("wt_ps"), g + 1)
                    nc.scalar.activation(wt, b3(1), ACT.Copy).then_inc(S("wt_sb"), 1)
                    act.wait_ge(S("ox_ps"), g + 1)
                    nc.scalar.activation(otmp, bank[4][:, 0:T], ACT.Copy).then_inc(S("ox_sb"), 1)
                    for i, (lo, hi) in enumerate(((0, 4), (4, 8), (8, 9))):
                        act.wait_ge(S("so_ps"), g * 3 + i + 1)
                        nc.scalar.activation(sout[:, lo:hi, :], bank[5 + i][0:HD, 0:(hi - lo) * P]
                                             .rearrange("p (i t) -> p i t", t=P), ACT.Copy).then_inc(S("so_sb"), 1)
                    act.wait_ge(S("o_ready"), g + 1)
                    act.wait_ge(S("so_sb"), g * 3 + 3)
                    act.sem_inc(S("pair_done"), 1)

            @block.vector
            def _(dve):
                ch = Chain(dve, S("pair_dve"))
                per = 12
                dve.sem_inc(S("pair_done"), 1)
                with dve.Fori(0, NPAIR) as g:
                    ch.n, ch.at = 0, g * per

                    def masked(b, dst, msk, ps, sb):
                        for h in range(2):
                            dve.wait_ge(S(ps), g * 2 + h + 1)
                            nc.vector.tensor_tensor(dst[:, h], b3(b[h]), msk, mult).then_inc(S(sb), 1)

                    def reduce_r(n, op, last=False):
                        for h in range(2):
                            dve.wait_ge(S("ap_ps"), g * 8 + 2 * n + h + 1)
                            if n == 0 and h == 0:
                                dve.wait_ge(S("al_sb"), g + 1)
                            v = rr[:, :, :, h, :]
                            nc.vector.tensor_tensor(v, v, b3(4 + h).rearrange("p j (a k) -> p j a k", a=2), op)\
                                .then_inc(S("r_ready" if last else "r_step"), 1)

                    masked((2, 3), x1t, m_st, "at_ps", "at_sb")
                    masked((4, 5), bt, m_st, "bt_ps", "bt_sb")
                    masked((6, 7), x1, m_ts, "a_m_ps", "a_m_sb")
                    reduce_r(0, sub)
                    masked((2, 3), ct, m_si, "ct_ps", "ct_sb")
                    dve.wait_ge(S("r_step"), g * 8 + 2)
                    reduce_r(1, add)
                    masked((2, 3), dt_, m_si, "dt_ps", "dt_sb")
                    dve.wait_ge(S("r_step"), g * 8 + 4)
                    reduce_r(2, add)
                    dve.wait_ge(S("r_step"), g * 8 + 6)
                    reduce_r(3, add, last=True)
                    dve.sem_inc(S("r_step"), 2)
                    dve.wait_ge(S("r_ready"), g * 2 + 2)
                    for q in range(2):
                        dve.wait_ge(S("us_ps"), g * 2 + q + 1)
                        nc.vector.tensor_tensor(us[:, 4 * q:4 * q + 4, :], bank[6 + q][:, :]
                                                .rearrange("p (b v) -> p b v", b=4),
                                                bc(rr[:, 2, 1].rearrange("p h v -> p (h v)"), 1, 4), add)\
                            .then_inc(S("us_raw"), 1)
                    dve.wait_ge(S("xm2_ready"), g + 1)
                    for c in range(NCH):
                        j, r, s = c // 8, slice(32 * (c % 8 // 2), 32 * (c % 8 // 2) + 32), c % 2
                        dve.wait_ge(S("u_ps"), g * NCH + c + 1)
                        nc.vector.scalar_tensor_tensor(out=um2[r, j, s, :], in0=bank[c % 2][r, 0:P],
                                                       scalar=cm2[r, s:s + 1], in1=xm2[r, j, s, :],
                                                       op0=mult, op1=add).then_inc(S("um_ready"), 1)
                        dve.wait_ge(S("s_ps"), g * NCH + c + 1)
                        for h in range(2):
                            d = slice(h * HD, (h + 1) * HD)
                            st = nc.vector.scalar_tensor_tensor(out=sbd[d, (c + 1) % 2, d], in0=sbd[d, c % 2, d],
                                                                scalar=ppend[d, c:c + 1], in1=bank[2 + c % 2][d, d],
                                                                op0=mult, op1=add)
                        st.then_inc(S("s_ready"), 1)
                    dve.wait_ge(S("us_ready"), g * 2 + 2)
                    ch(nc.vector.tensor_reduce(ut, us.rearrange("p b v -> p v b"), AX.X, add))
                    dve.wait_ge(S("uu_raw"), g + 1)
                    nc.vector.tensor_tensor(uu[:, 2, :], uu[:, 2, :], ut, add).then_inc(S("uu_ready"), 1)
                    dve.wait_ge(S("s_ready"), g * NCH + NCH)
                    for h in range(2):
                        d = slice(h * HD, (h + 1) * HD)
                        ch(nc.vector.tensor_copy(snew[d, 0, :], sbd[d, NCH % 2, d]))
                        ch(nc.vector.tensor_tensor(snew[d, 1:, :], s0bd[d, :, d], bc(ppend[d, NCH:], 2, HD), mult))
                        for q in range(2):
                            dve.wait_ge(S("sn_ps"), g * 2 + q + 1)
                            v = snew[d, 1 + 4 * q:5 + 4 * q, :]
                            ch(nc.vector.tensor_tensor(v, v, bank[6 + q][d, :].rearrange("p (b v) -> p b v", b=4)[:, :, d],
                                                       add))
                    dve.sem_inc(S("snew_ready"), 1)
                    dve.wait_ge(S("ocd_ps"), g + 1)
                    dve.wait_ge(S("ox_sb"), g + 1)
                    for j, n in enumerate(ROWS):
                        c = slice(j * P, j * P + n)
                        o = nc.vector.tensor_tensor(ar[:, AL, bass.ds(g, 1), c].rearrange("p a t -> p (a t)"),
                                                    bank[j][:, 0:n], otmp[:, c], add)
                        if j < NT - 1:
                            ch(o)
                    ch(o)
                    dve.sem_inc(S("o_ready"), 1)
                    assert ch.n == per, ch.n

        retire()

        low = Space(arena, base, base + ATILES * ZC)
        oo = low(NPAIR, T)
        osq = low(NPAIR, T)
        oT = lambda g: ar[:, AL, g, 0:T]
        with nc.Block("rwkv_post") as block:
            @block.tensor
            def _(pe):
                for g in range(NPAIR):
                    nc.tensor.matmul(bank[g][:, 0:T], headones, oT(g), start=True, stop=True)\
                        .then_inc(S("om_ps"), 1)
                for g in range(NPAIR):
                    pe.wait_ge(S("osq_ready"), g + 1)
                    nc.tensor.matmul(bank[4 + g][:, 0:T], headones, osq[:, g, :], start=True, stop=True)\
                        .then_inc(S("ov_ps"), 1)

            @block.scalar
            def _(act):
                for g in range(NPAIR):
                    act.wait_ge(S("oc_ready"), g + 1)
                    nc.scalar.activation(osq[:, g, :], oo[:, g, :], ACT.Square).then_inc(S("osq_ready"), 1)
                act.wait_ge(S("ov_ready"), 1)
                nc.scalar.activation(osq, osq, ACT.Sqrt).then_inc(S("ort_ready"), 1)

            @block.vector
            def _(dve):
                ch = Chain(dve, S("post_dve"))
                for g in range(NPAIR):
                    dve.wait_ge(S("om_ps"), g + 1)
                    nc.vector.scalar_tensor_tensor(out=oo[:, g, :], in0=bank[g][:, 0:T], scalar=-1.0 / HD, in1=oT(g),
                                                   op0=mult, op1=add).then_inc(S("oc_ready"), 1)
                dve.wait_ge(S("oc_ready"), 4)
                for g in range(NPAIR):
                    dve.wait_ge(S("ov_ps"), g + 1)
                    ch(nc.vector.tensor_scalar(osq[:, g, :], bank[4 + g][:, 0:T], 1.0 / HD, GN_EPS, mult, add))
                dve.sem_inc(S("ov_ready"), 1)
                dve.wait_ge(S("ort_ready"), 1)
                ch(nc.vector.reciprocal(f4(osq), f4(osq)))
                ch(nc.vector.tensor_tensor(oo, oo, osq, mult))
                for g in range(NPAIR):
                    ch(nc.vector.tensor_scalar(oo[:, g, :], oo[:, g, :], prm[:, LNW + g:LNW + g + 1],
                                               prm[:, LNB + g:LNB + g + 1], mult, add))
                ch(nc.vector.tensor_tensor(oo, oo, bonus, add))
                ch(nc.vector.tensor_tensor(gate, gate, oo, mult))

        retire()

        sp5 = Space(arena, base + ATILES * ZC + NPAIR * T, NF)
        QC = NH * DS
        G4 = 4 * P
        lfg = sp5(PAGE * NH)
        lfT = sp5(NH, DB * NPAGES)
        later = sp5(NH, DB * NPAGES)
        rsuf = sp5(NH, DB, NPAGES)
        tri_key = sp5(P)
        kT = sp5(2, NPAIR, G4)
        rbc = sp5(NPAGES, QC)
        pp = sp5(NPAGES * PAGE + DS, parts=QC)
        pT = sp5(NPAGES, QC)
        pTn = sp5(QC, parts=DS)
        osb = sp5(BW, parts=QC)
        mx, nm, sums, rs, rsp = (sp5(n, parts=QC) for n in (5, 1, 5, 1, 1))
        qcur = sp5(NPAIR * (QC + 2 * DS))
        kcur = sp5(NPAIR, DS)
        nmcur = sp5(QC, parts=DS)
        vcur = sp5(BW, parts=DS)
        assert QC == HD
        NEW = 256
        fills = [16 * (1 + (s in aslots)) if s < 6 else 16 for s in range(SLOTS)]
        TURN, SC, PVS = NPAGES + 2, 5, 5
        EVEN = TURN // 2
        kT_sem = ("kT_even", "kT_odd")

        with nc.Block("cache") as block:
            @block.sync
            def _(sp):
                def keys_of(b, after):
                    for s in range(4):
                        pages = page_numbers(sp, s, b)
                        sp.wait_ge(S("kT_ps"), after * TURN + 4 * s + 4)
                        load_pages(sp, s, pages)

                def values_of(b):
                    for s in range(4, SLOTS):
                        pages = page_numbers(sp, s, b)
                        sp.wait_ge(S("pv_ps"), (b - 1) * PVS + s - 3)
                        load_pages(sp, s, pages)
                    sp.wait_ge(S("pv_ps"), b * PVS)

                sp.dma_start(vcur, A_vs[0]).then_inc(S("vcur_in"), 16)
                keys_of(1, 0)
                with sp.Fori(0, DB - 2) as i:
                    keys_of(i + 2, i + 1)
                    values_of(i + 1)
                    sp.dma_start(vcur, A_vs[bass.ds(i + 1, 1)].rearrange("a t n -> (a t) n")).then_inc(S("vcur_in"), 16)
                for n in range(4):
                    sp.wait_ge(S("kT_ps"), (DB - 1) * TURN + 4 * n + 4)
                    sp.dma_start(slot[n], merge_load(n)).then_inc(full[n], 16)
                values_of(DB - 1)
                sp.dma_start(vcur, A_vs[DB - 1]).then_inc(S("vcur_in"), 16)
                for n in range(4, SLOTS):
                    sp.wait_ge(S("pv_ps"), (DB - 1) * PVS + n - 3)
                    sp.dma_start(slot[n], merge_load(n)).then_inc(full[n], 16)

            @block.gpsimd
            def _(pool):
                ch = Chain(pool, S("cache_pool"))
                nc.gpsimd.indirect_dma_start(lfg, None, A["clf"], bass.IndirectOffsetOnAxis(ap=pt_col[:, 0:1], axis=0))\
                    .then_inc(S("lfg_in"), 16)
                ch(nc.gpsimd.memset(tri_key, 1.0))
                ch(nc.gpsimd.affine_select(out=tri_key, in_=tri_key, compare_op=ALU.is_gt, fill=0.0, base=0,
                                           pattern=[[-1, P]], channel_multiplier=1))
                pool.sem_inc(S("tri_ready"), 1)
                ch(nc.gpsimd.memset(qcur, 0.0))
                pool.wait_ge(S("rsuf_sb"), 2)
                start, per = ch.n, 4
                with pool.Fori(0, DB) as b:
                    ch.n, ch.at = 0, b * per + start
                    pool.wait_ge(S("sc_ps"), b * SC + SC)
                    ch(nc.gpsimd.tensor_copy(qcur.rearrange("p (g c) -> p g c", g=NPAIR)[:, :, 0:2 * DS],
                                             q_all[:, bass.ds(b, 1)].rearrange("p a g q -> p (a g) q")))
                    ch(nc.gpsimd.tensor_copy(kcur, knT[:, :, bass.ds(b * DS, DS)]))
                    ch(nc.gpsimd.tensor_copy(nmcur, newmask[:, bass.ds(b, 1)].rearrange("p a h q -> p (a h q)")))
                    ch(nc.gpsimd.tensor_copy(rbc.rearrange("p n (h q) -> p n h q", h=NH),
                                             bc(rsuf[:, :, bass.ds(b, 1), :].rearrange("p h a n -> p n (h a)"), 3, DS)))
                    pool.sem_inc(S("cur_ready"), 1)
                    assert ch.n == per

            @block.tensor
            def _(pe):
                pe.sem_inc(S("sc_ps"), SC)
                pe.wait_ge(S("lfg_in"), 16)
                lv = lfg.rearrange("p (k h) -> p k h", h=NH)
                for h in range(NH):
                    mm = nc.tensor.transpose(bank[h // 4][:, (h % 4) * P:(h % 4 + 1) * P], lv[:, :, h], ident)
                    if h % 4 == 3:
                        mm.then_inc(S("lfT_ps"), 1)
                pe.wait_ge(S("tri_ready"), 1)
                pe.wait_ge(S("later_ready"), 1)
                for q in range(2):
                    nc.tensor.matmul(bank[2 + q][:, :], tri_key, lfT[:, 4 * q:4 * q + 4, :].rearrange("p h n -> p (h n)"),
                                     start=True, stop=False)
                    nc.tensor.matmul(bank[2 + q][:, :], ones, later[:, 4 * q:4 * q + 4, :].rearrange("p h n -> p (h n)"),
                                     start=False, stop=True).then_inc(S("rsuf_ps"), 1)
                pe.wait_ge(S("rsuf_sb"), 2)

                def turn(b, n):
                    if n % 4 == 0:
                        pe.wait_ge(full[n // 4], fills[n // 4] + (b + 1) * 64)
                    pe.wait_ge(S(kT_sem[n % 2]), b * EVEN + n // 2 + 1)
                    for g in range(NPAIR):
                        mm = nc.tensor.transpose(bank[n % 2][:, g * P:(g + 1) * P],
                                                 slot[n // 4][:, (n % 4) * BW + g * P:(n % 4) * BW + (g + 1) * P], ident)
                    mm.then_inc(S("kT_ps"), 1)

                def all_scores(b, first=False):
                    for n in range(4):
                        turn(b, n)
                    pe.wait_ge(S("cur_ready"), b + 1)
                    for m in range(4):
                        for s in kT_sem:
                            pe.wait_ge(S(s), b * EVEN + 2 * m + 3)
                        pe.wait_ge(S("exp_out"), b * SC + m + 1)
                        for g in range(NPAIR):
                            nc.tensor.matmul(bank[2 + m][0:QC, :], qcur[:, g * QC:(g + 1) * QC], kT[:, m % 2, g, :],
                                             start=(g == 0), stop=False, skip_group_check=True)
                            if m < 3:
                                turn(b, 4 * m + 4 + g)
                        for n in range(4):
                            mm = nc.tensor.matmul(bank[2 + m][0:QC, n * P:(n + 1) * P], rbc[:, 4 * m + n, :], ident,
                                                  start=False, stop=True, skip_group_check=True)
                        mm.then_inc(S("sc_ps"), 1)
                    pe.wait_ge(S("exp_out"), b * SC + 5)
                    if not first:
                        pe.wait_ge(S("ob_out"), b)
                    for g in range(NPAIR):
                        nc.tensor.matmul(bank[6][0:QC, NEW:NEW + DS], qcur[:, g * QC:(g + 1) * QC], kcur[:, g, :],
                                         start=(g == 0), stop=False)
                    nc.tensor.matmul(bank[6][0:QC, NEW:NEW + DS], nmcur, ident[0:DS, 0:DS], start=False, stop=True)\
                        .then_inc(S("sc_ps"), 1)

                def turn_probs(b):
                    for j in range(2):
                        pe.wait_ge(S(kT_sem[j]), b * EVEN + EVEN)
                        pe.wait_ge(S("exp_out"), b * SC + 2 * SC)
                        for n in range(8):
                            o = bank[j][:, n * QC:(n + 1) * QC]
                            i = pp[:, (8 * j + n) * P:(8 * j + n + 1) * P]
                            if n == 0:
                                nc.tensor.matmul(o, i, ident[0:QC, 0:QC], start=True, stop=True)
                            else:
                                mm = nc.tensor.transpose(o, i, ident[0:QC, 0:QC])
                        mm.then_inc(S("kT_ps"), 1)
                    nc.tensor.transpose(bank[6][0:DS, NEW + DS:NEW + DS + QC], pp[:, NPAGES * P:], ident[0:QC, 0:QC])\
                        .then_inc(S("pn_ps"), 1)

                def weigh(b):
                    for s in kT_sem:
                        pe.wait_ge(S(s), b * EVEN + EVEN + 1)
                    pe.wait_ge(S("pn_sb"), b + 1)
                    pe.wait_ge(S("o_sb"), b + 1)
                    for n in range(NPAGES):
                        s = 4 + n // 4
                        if n % 4 == 0:
                            pe.wait_ge(full[s], fills[s] + (b + 1) * 64)
                        mm = nc.tensor.matmul(bank[7][0:QC, :], pT[:, n, :], slot[s][:, (n % 4) * BW:(n % 4 + 1) * BW],
                                              start=(n == 0), stop=False)
                        if n % 4 == 3:
                            mm.then_inc(S("pv_ps"), 1)
                    pe.wait_ge(S("vcur_in"), (b + 1) * 16)
                    nc.tensor.matmul(bank[7][0:QC, :], pTn, vcur, start=False, stop=True).then_inc(S("pv_ps"), 1)

                def turn_out(b, last=False):
                    if not last:
                        pe.wait_ge(S("pn_sb"), b + 2)
                    pe.wait_ge(S("ob_out"), b + 1)
                    pe.wait_ge(S("o_sb"), b + 2)
                    for g in range(NPAIR):
                        o, i = bank[6][:, g * QC:(g + 1) * QC], osb[:, g * P:(g + 1) * P]
                        if g == 0:
                            nc.tensor.matmul(o, i, ident[0:QC, 0:QC], start=True, stop=True)
                        else:
                            mm = nc.tensor.transpose(o, i, ident[0:QC, 0:QC])
                    mm.then_inc(S("oT_ps"), 1)

                all_scores(0, first=True)
                turn_probs(0)
                with pe.Fori(0, DB - 1) as i:
                    all_scores(i + 1)
                    weigh(i)
                    turn_probs(i + 1)
                    turn_out(i)
                weigh(DB - 1)
                turn_out(DB - 1, last=True)

            @block.scalar
            def _(act):
                act.sem_inc(S("kT_even"), 1)
                act.sem_inc(S("exp_out"), SC)
                for q in range(2):
                    act.wait_ge(S("lfT_ps"), q + 1)
                    nc.scalar.activation(lfT[:, 4 * q:4 * q + 4, :], bank[q][:, :].rearrange("p (h n) -> p h n", h=4),
                                         ACT.Copy).then_inc(S("lfT_sb"), 1)
                for q in range(2):
                    act.wait_ge(S("rsuf_ps"), q + 1)
                    nc.scalar.activation(rsuf[:, 4 * q:4 * q + 4].rearrange("p h b n -> p (h b n)"), bank[2 + q][:, :],
                                         ACT.Copy).then_inc(S("rsuf_sb"), 1)

                def sample(b, first=False):
                    for n in range(0, NPAGES, 2):
                        m = n // 4
                        act.wait_ge(S("kT_ps"), b * TURN + n + 1)
                        act.wait_ge(S("sc_ps"), b * SC + (SC + m - 1 if m >= 2 else m + 3))
                        nc.scalar.activation(kT[:, m % 2, :, (n % 4) * P:(n % 4 + 1) * P],
                                             bank[0][:, :].rearrange("p (g k) -> p g k", g=NPAIR), ACT.Copy)\
                            .then_inc(S("kT_even"), 1)
                    act.wait_ge(S("nm_ready"), b + 1)
                    act.wait_ge(S("sums_used"), b + 1)
                    if not first:
                        act.wait_ge(S("pn_ps"), b)
                    for m in range(SC):
                        src = bank[2 + m][0:QC, :] if m < 4 else bank[6][0:QC, NEW:NEW + DS]
                        dst = pp[:, m * G4:(m + 1) * G4] if m < 4 else pp[:, 4 * G4:]
                        nc.scalar.activation(dst, src, ACT.Exp, bias=nm[:, 0:1], accum_out=sums[:, m:m + 1])\
                            .then_inc(S("exp_out"), 1)
                    act.wait_ge(S("kT_ps"), b * TURN + NPAGES + 1)
                    if not first:
                        act.wait_ge(S("pv_ps"), b * PVS)
                    nc.scalar.activation(pT[:, 0:8, :].rearrange("p n c -> p (n c)"), bank[0][:, :], ACT.Copy)\
                        .then_inc(S("kT_even"), 1)

                sample(0, first=True)
                with act.Fori(0, DB - 1) as i:
                    sample(i + 1)

            @block.vector
            def _(dve):
                ch = Chain(dve, S("cache_dve"))
                for s in ("kT_odd", "sums_used", "o_sb", "ob_out"):
                    dve.sem_inc(S(s), 1)
                lt = later.rearrange("p h (b n) -> p (h b) n", n=NPAGES)
                lf_ = lfT.rearrange("p h (b n) -> p (h b) n", n=NPAGES)
                ch(nc.vector.memset(rs, 0.0))
                ch(nc.vector.memset(lt[:, :, NPAGES - 1], 0.0))
                dve.wait_ge(S("lfT_sb"), 2)
                for n in range(NPAGES - 2, -1, -1):
                    ch(nc.vector.tensor_tensor(lt[:, :, n], lt[:, :, n + 1], lf_[:, :, n + 1], add))
                dve.sem_inc(S("later_ready"), 1)

                def softmax(b):
                    def top(m):
                        dve.wait_ge(S("sc_ps"), b * SC + SC + m + 1)
                        src = bank[2 + m][0:QC, :] if m < 4 else bank[6][0:QC, NEW:NEW + DS]
                        ch(nc.vector.tensor_reduce(mx[:, m:m + 1], src, AX.X, vmax))

                    for n in range(1, NPAGES, 2):
                        m = n // 4
                        dve.wait_ge(S("kT_ps"), b * TURN + n + 1)
                        dve.wait_ge(S("sc_ps"), b * SC + (SC + m - 1 if m >= 2 else m + 3))
                        nc.vector.tensor_copy(kT[:, m % 2, :, (n % 4) * P:(n % 4 + 1) * P],
                                              bank[1][:, :].rearrange("p (g k) -> p g k", g=NPAIR))\
                            .then_inc(S("kT_odd"), 1)
                        if n in (9, 13):
                            top((n - 9) // 4)
                    for m in (2, 3, 4):
                        top(m)
                    ch(nc.vector.tensor_reduce(nm, mx, AX.X, vmax))
                    ch(nc.vector.tensor_scalar(nm, nm, -1.0, None, mult))
                    dve.sem_inc(S("nm_ready"), 1)
                    ch(nc.vector.tensor_copy(rsp, rs))
                    dve.wait_ge(S("exp_out"), b * SC + 2 * SC)
                    ch(nc.vector.tensor_reduce(rs, sums, AX.X, add))
                    dve.sem_inc(S("sums_used"), 1)
                    ch(nc.vector.reciprocal(rs, rs))

                def scale_out(b, r):
                    dve.wait_ge(S("pv_ps"), b * PVS + PVS)
                    nc.vector.tensor_scalar(osb, bank[7][0:QC, :], r[:, 0:1], None, mult).then_inc(S("o_sb"), 1)

                def probs(b):
                    dve.wait_ge(S("kT_ps"), b * TURN + TURN)
                    nc.vector.tensor_copy(pT[:, 8:16, :].rearrange("p n c -> p (n c)"), bank[1][:, :])\
                        .then_inc(S("kT_odd"), 1)
                    dve.wait_ge(S("pn_ps"), b + 1)
                    nc.vector.tensor_copy(pTn, bank[6][0:DS, NEW + DS:NEW + DS + QC]).then_inc(S("pn_sb"), 1)

                def keep_out(b):
                    dve.wait_ge(S("oT_ps"), b + 1)
                    for e in range(2):
                        r = slice(e * HD, (e + 1) * HD)
                        v = bank[6][r, 0:NPAIR * (QC + 2 * DS)].rearrange("p (g c) -> p g c", g=NPAIR)
                        o = nc.vector.tensor_copy(obT[r, :, bass.ds(b * DS + LP, DS)], v[:, :, e * DS:(e + 1) * DS])
                        if e == 0:
                            ch(o)
                    ch(o)
                    dve.sem_inc(S("ob_out"), 1)

                SOFT, OUT = SC + 5, 2
                n0 = ch.n
                softmax(0)
                probs(0)
                assert ch.n == n0 + SOFT
                start = ch.n
                with dve.Fori(0, DB - 1) as i:
                    ch.n, ch.at = 0, i * (SOFT + OUT) + start
                    softmax(i + 1)
                    scale_out(i, rsp)
                    probs(i + 1)
                    keep_out(i)
                    assert ch.n == SOFT + OUT
                ch.at, ch.n = (DB - 1) * (SOFT + OUT) + start, 0
                scale_out(DB - 1, rs)
                keep_out(DB - 1)

        retire()

        sp6 = Space(arena, base + ATILES * ZC + NPAIR * T, NF)
        h2 = sp6(NT, DM)
        mark6 = sp6.at
        mT = sp6(KT, T)
        xt6 = sp6(NT, DM)
        sga, sgb, tga, tgb = (sp6(2, T) for _ in range(4))
        mfills = [fills[s] + 64 * DB for s in range(SLOTS)]
        ND = DM // P
        WO = 12

        with nc.Block("merge") as block:
            @block.sync
            def _(sp):
                sp.dma_start(xt6[0:NMETA, 0, :], A["meta"]).then_inc(S("xr_in"), 16)
                sp.dma_start(xt6[NMETA:P, 0, :], A["xp"][0:P - NMETA, :]).then_inc(S("xr_in"), 16)
                sp.dma_start(xt6[:, 1, :], A["xp"][P - NMETA:2 * P - NMETA, :]).then_inc(S("xr_in"), 16)
                sp.dma_start(xt6[0:NMETA, 2, :], A["xp"][2 * P - NMETA:SEQ, :]).then_inc(S("xr_in"), 16)
                sp.dma_start(xt6[NMETA:ROWS[2], 2, :], A["xs"]).then_inc(S("xr_in"), 16)
                for n in range(SLOTS, WO + 4):
                    dd, part = divmod(n - SLOTS, 3)
                    sp.wait_ge(S("mg_ps"), 8 * dd + (2, 6, 8)[part])
                    sp.dma_start(slot[n % SLOTS], merge_load(n)).then_inc(full[n % SLOTS], 16)

            @block.tensor
            def _(pe):
                def have(n):
                    pe.wait_ge(full[n % SLOTS], mfills[n % SLOTS] + 16 * (n // SLOTS + 1))

                for d in range(ND):
                    b0 = 4 * (d % 2)
                    n = 3 * (d // 2) + d % 2
                    have(n)
                    if d >= 2:
                        pe.wait_ge(S("sgm_sb"), 2 * (d - 2) + 2)
                        pe.wait_ge(S("tg_sb"), 2 * (d - 2) + 2)
                    w = slot[n % SLOTS].rearrange("p (k a n) -> p k a n", k=KT, a=2)
                    for a in range(2):
                        for k in range(KT):
                            mm = nc.tensor.matmul(bank[b0 + a][:, 0:T], w[:, k, a, :], xnT[:, k, :],
                                                  start=(k == 0), stop=(k == KT - 1))
                        mm.then_inc(S("mg_ps"), 1)
                    n = 3 * (d // 2) + 2
                    have(n)
                    w = slot[n % SLOTS].rearrange("p (d a k n) -> p d a k n", d=2, a=2, k=4)
                    for a, src in enumerate((gate, obT)):
                        for k in range(4):
                            mm = nc.tensor.matmul(bank[b0 + 2 + a][:, 0:T], w[:, d % 2, a, k, :], src[:, k, :],
                                                  start=(k == 0), stop=(k == 3))
                        mm.then_inc(S("mg_ps"), 1)
                pe.wait_ge(S("m_ready"), ND)
                for k in range(KT):
                    n = WO + k // 2
                    if k % 2 == 0:
                        have(n)
                    w = slot[n % SLOTS].rearrange("p (k n) -> p k n", k=2)
                    for i, r in enumerate(ROWS):
                        for half in range(2):
                            mm = nc.tensor.matmul(bank[2 * i + half][0:r, :], mT[:, k, i * P:i * P + r],
                                                  w[:, k % 2, half * 512:(half + 1) * 512],
                                                  start=(k == 0), stop=(k == KT - 1))
                            if k == KT - 1:
                                mm.then_inc(S("ho_ps"), 1)

            @block.scalar
            def _(act):
                for d in range(ND):
                    b0 = 4 * (d % 2)
                    if d >= 2:
                        act.wait_ge(S("tg_sb"), 2 * (d - 2) + 2)
                    for a, sgx in enumerate((sga, sgb)):
                        act.wait_ge(S("mg_ps"), 4 * d + a + 1)
                        nc.scalar.activation(sgx[:, d % 2, :], bank[b0 + a][:, 0:T], ACT.Sigmoid)\
                            .then_inc(S("sgm_sb"), 1)

            @block.gpsimd
            def _(pool):
                for d in range(ND):
                    pool.wait_ge(S("tg_sb"), 2 * d + 2)
                    nc.gpsimd.tensor_tensor(mT[:, d, :], tga[:, d % 2, :], tgb[:, d % 2, :], add)\
                        .then_inc(S("m_ready"), 1)

            @block.vector
            def _(dve):
                for d in range(ND):
                    b0 = 4 * (d % 2)
                    if d >= 2:
                        dve.wait_ge(S("m_ready"), d - 1)
                    for a, (sgx, tgx) in enumerate(((sga, tga), (sgb, tgb))):
                        dve.wait_ge(S("sgm_sb"), 2 * d + a + 1)
                        dve.wait_ge(S("mg_ps"), 4 * d + 2 + a + 1)
                        nc.vector.tensor_tensor(tgx[:, d % 2, :], bank[b0 + 2 + a][:, 0:T], sgx[:, d % 2, :], mult)\
                            .then_inc(S("tg_sb"), 1)
                dve.wait_ge(S("xr_in"), 80)
                for i, r in enumerate(ROWS):
                    for half in range(2):
                        c = slice(half * 512, (half + 1) * 512)
                        dve.wait_ge(S("ho_ps"), 2 * i + half + 1)
                        nc.vector.tensor_tensor(h2[0:r, i, c], bank[2 * i + half][0:r, :], xt6[0:r, i, c], add)

        retire()

        sp7 = Space(arena, mark6, NF)
        x2 = sp7(NT, DM)
        x2T = xnT
        lnb2 = sp7(DM)
        wr = sp7(KT, NG + NE)
        lg = sp7(NT, NG + NE)
        desc = sp7(EPG)
        iop = sp7(8)
        iot = sp7(P)
        tokmask = sp7(NT)
        ohg, w4, eg = (sp7(NT, NG) for _ in range(3))
        el = sp7(NT, NG, EPG)
        sel, sel2, w8, oh1, oh2, cw = (sp7(NT, EPG) for _ in range(6))
        gm, gs, gp, m1, m2, wm, e12, wa, wb, dest, dtmp = (sp7(NT) for _ in range(11))
        cnt = sp7(NT, NG)
        tot, nb, nbt = sp7(NG), sp7(NG), sp7(NG)
        pb = sp7(NG + 1)
        gop, gopt = sp7(8), sp7(8)
        mark7 = sp7.at
        ss, ms, rt, rstd = (small[:, i * NT:(i + 1) * NT] for i in range(4))
        jk = sp7(NT, DM)
        np_i = ctx.enter_context(nc.sbuf_tensor("np_i", [1, 1], i32))
        gop_i = ctx.enter_context(nc.sbuf_tensor("gop_i", [1, 8], i32))
        MAXPASS = NG + (T - NMETA) // P

        with nc.Block("route") as block:
            @block.sync
            def _(sp):
                sp.dma_start(lnb2, ln_row[1, :].partition_broadcast(P)).then_inc(S("ln2_in"), 16)
                sp.dma_start(wr, A["w_r"]).then_inc(S("wr_in"), 16)

            @block.gpsimd
            def _(pool):
                ch = Chain(pool, S("route_pool"))
                for i in range(8):
                    ch(nc.gpsimd.memset(desc[:, i:i + 1], float(EPG - i)))
                    ch(nc.gpsimd.memset(iop[:, i:i + 1], float(i)))
                ch(nc.gpsimd.iota(iot, pattern=[[1, P]], base=0, channel_multiplier=0,
                                  allow_small_or_imprecise_dtypes=True))
                ch(nc.gpsimd.memset(tokmask, 1.0))
                for pat, b, m in (([[P, NT]], -NMETA, 1), ([[-P, NT]], T - 1, -1)):
                    ch(nc.gpsimd.affine_select(out=tokmask, in_=tokmask, compare_op=ALU.is_ge, fill=0.0, base=b,
                                               pattern=pat, channel_multiplier=m))
                pool.sem_inc(S("rconst"), 1)

            @block.scalar
            def _(act):
                act.wait_ge(S("rz"), 1)
                for i, n in enumerate(ROWS):
                    nc.scalar.activation(jk[0:n, i, :], h2[0:n, i, :], ACT.Square,
                                         accum_out=ss[0:n, i:i + 1]).then_inc(S("ss2"), 1)
                act.wait_ge(S("ms2"), 1)
                nc.scalar.activation(rt, ms, ACT.Sqrt).then_inc(S("rt2"), 1)
                for i, n in enumerate(ROWS):
                    act.wait_ge(S("x2T_ps"), 2 * i + 2)
                    nc.scalar.activation(x2T[:, 4:8, i * P:i * P + n],
                                         bank[2 * i + 1][:, :].rearrange("p (k t) -> p k t", k=4)[:, :, 0:n],
                                         ACT.Copy).then_inc(S("x2T_b"), 1)
                act.wait_ge(S("eg_in"), 1)
                nc.scalar.activation(eg, eg, ACT.Exp).then_inc(S("eg_out"), 1)
                act.wait_ge(S("e12_in"), 1)
                nc.scalar.activation(e12, e12, ACT.Exp).then_inc(S("e12_out"), 1)

            @block.tensor
            def _(pe):
                for i, n in enumerate(ROWS):
                    pe.wait_ge(S("x2_ready"), i + 1)
                    for half in range(2):
                        for k in range(4):
                            kk = 4 * half + k
                            mm = nc.tensor.transpose(bank[2 * i + half][:, k * P:k * P + n],
                                                     x2[0:n, i, kk * P:(kk + 1) * P], ident[0:n, 0:n])
                        mm.then_inc(S("x2T_ps"), 1)
                pe.wait_ge(S("wr_in"), 16)
                pe.wait_ge(S("x2T_a"), 3)
                pe.wait_ge(S("x2T_b"), 3)
                E_ = NG + NE
                for i, n in enumerate(ROWS):
                    for k in range(KT):
                        mm = nc.tensor.matmul(bank[6][0:n, i * E_:(i + 1) * E_], x2T[:, k, i * P:i * P + n], wr[:, k, :],
                                              start=(k == 0), stop=(k == KT - 1))
                mm.then_inc(S("lg_ps"), 1)
                pe.wait_ge(S("ohg_ready"), 1)
                for i in range(NT):
                    for k in range(i + 1):
                        nc.tensor.matmul(bank[7][:, i * NG:(i + 1) * NG], tri_tok if k == i else ones, ohg[:, k, :],
                                         start=(k == 0), stop=(k == i))
                for k in range(NT):
                    mm = nc.tensor.matmul(bank[7][:, NT * NG:(NT + 1) * NG], ones, ohg[:, k, :],
                                          start=(k == 0), stop=(k == NT - 1))
                mm.then_inc(S("cnt_ps"), 1)

            @block.vector
            def _(dve):
                ch = Chain(dve, S("route_dve"))
                TT, TS, STT, TR = (nc.vector.tensor_tensor, nc.vector.tensor_scalar, nc.vector.scalar_tensor_tensor,
                                   nc.vector.tensor_reduce)
                eq = ALU.is_equal
                ch(nc.vector.memset(ss, 1.0))
                dve.sem_inc(S("rz"), 1)
                ch(nc.vector.memset(x2[:, 2, :], 0.0))
                ch(nc.vector.memset(lg, 0.0))
                dve.wait_ge(S("ss2"), 3)
                ch(TS(ms, ss, 1.0 / DM, RMS_EPS, mult, add))
                dve.sem_inc(S("ms2"), 1)
                dve.wait_ge(S("rt2"), 1)
                ch(nc.vector.reciprocal(rstd, rt))
                dve.wait_ge(S("ln2_in"), 16)
                for i, n in enumerate(ROWS):
                    STT(out=x2[0:n, i, :], in0=h2[0:n, i, :], scalar=rstd[0:n, i:i + 1], in1=lnb2[0:n, :],
                        op0=mult, op1=mult).then_inc(S("x2_ready"), 1)
                for i, n in enumerate(ROWS):
                    dve.wait_ge(S("x2T_ps"), 2 * i + 1)
                    nc.vector.tensor_copy(x2T[:, 0:4, i * P:i * P + n],
                                          bank[2 * i][:, :].rearrange("p (k t) -> p k t", k=4)[:, :, 0:n])\
                        .then_inc(S("x2T_a"), 1)
                dve.wait_ge(S("lg_ps"), 1)
                for i, n in enumerate(ROWS):
                    ch(nc.vector.tensor_copy(lg[0:n, i, :], bank[6][0:n, i * (NG + NE):(i + 1) * (NG + NE)]))
                dve.wait_ge(S("rconst"), 1)

                def first(x, m, d, w, oh):
                    ch(TT(w, x, bc(m, 2, x.shape[2]), eq))
                    ch(TT(w, w, bc(d, 1, NT), mult))
                    ch(TR(wm, w, AX.X, vmax))
                    ch(TT(oh, w, bc(wm, 2, x.shape[2]), eq))

                g4 = lg[:, :, 0:NG]
                ch(TR(gm, g4, AX.X, vmax))
                ch(TT(eg, g4, bc(gm, 2, NG), sub))
                dve.sem_inc(S("eg_in"), 1)
                first(g4, gm, desc[:, EPG - NG:EPG], w4, ohg)
                ch(TT(ohg, ohg, bc(tokmask, 2, NG), mult))
                dve.sem_inc(S("ohg_ready"), 1)
                dve.wait_ge(S("eg_out"), 1)
                ch(TR(gs, eg, AX.X, add))
                ch(nc.vector.reciprocal(gp, gs))
                ch(TT(el, lg[:, :, NG:].rearrange("p i (g e) -> p i g e", g=NG), bc(ohg, 3, EPG), mult))
                ch(TR(sel, el.rearrange("p i g e -> p i e g"), AX.X, add))
                ch(TR(m1, sel, AX.X, vmax))
                first(sel, m1, desc, w8, oh1)
                ch(STT(out=sel2, in0=oh1, scalar=NEG, in1=sel, op0=mult, op1=add))
                ch(TR(m2, sel2, AX.X, vmax))
                first(sel2, m2, desc, w8, oh2)
                ch(TT(e12, m2, m1, sub))
                dve.sem_inc(S("e12_in"), 1)
                dve.wait_ge(S("e12_out"), 1)
                ch(TS(wa, e12, 1.0, None, add))
                ch(nc.vector.reciprocal(wa, wa))
                ch(TT(wa, wa, gp, mult))
                ch(TT(wb, wa, e12, mult))
                ch(TT(cw, oh1, bc(wa, 2, EPG), mult))
                ch(TT(oh2, oh2, bc(wb, 2, EPG), mult))
                ch(TT(cw, cw, oh2, add))
                dve.wait_ge(S("cnt_ps"), 1)
                ch(nc.vector.tensor_copy(cnt, bank[7][:, 0:NT * NG].rearrange("p (i g) -> p i g", g=NG)))
                ch(nc.vector.tensor_copy(tot, bank[7][:, NT * NG:(NT + 1) * NG]))
                ch(TS(nb, tot, 0.0, None, ALU.is_gt))
                for k in range(1, NT):
                    ch(TS(nbt, tot, float(k * P), None, ALU.is_gt))
                    ch(TT(nb, nb, nbt, add))
                ch(nc.vector.memset(pb[:, 0:1], 0.0))
                for k in range(NG):
                    ch(TT(pb[:, k + 1:k + 2], pb[:, k:k + 1], nb[:, k:k + 1], add))
                ch(TS(gop, iop, pb[:, 1:2], None, ALU.is_ge))
                for k in range(2, NG):
                    ch(TS(gopt, iop, pb[:, k:k + 1], None, ALU.is_ge))
                    ch(TT(gop, gop, gopt, add))
                ch(nc.vector.tensor_copy(gop_i[:, :], gop[0:1, :]))
                ch(nc.vector.tensor_copy(np_i[:, :], pb[0:1, NG:NG + 1]))
                ch(TS(pb[:, 0:NG], pb[:, 0:NG], float(P), 1.0, mult, add))
                ch(TT(cnt, cnt, bc(pb[:, 0:NG], 1, NT), add))
                ch(TT(cnt, cnt, ohg, mult))
                ch(TR(dest, cnt, AX.X, add))
                ch(TS(dest, dest, -1.0, None, add))

        retire()

        sp8 = Space(arena, mark7, NF)
        gsel = sp8(NT, P)
        gT = sp8(NT, P)
        xg = sp8(KT, P)
        cwg = sp8(EPG)
        sig, hid = sp8(2, FF), sp8(2, FF)
        hT = sp8(2, 2, P)
        yg = sp8(DM)
        zrow = sp8(512, parts=1)
        EH = EPG // 2
        wfull = lambda j, part: S(f"w_full{j}{part}")

        with nc.Block("moe") as block:
            @block.sync
            def _(sp):
                n_pass = sp.value_load(np_i[0:1, 0:1], min_val=1, max_val=MAXPASS)
                with sp.Fori(0, n_pass) as p:
                    grp = sp.value_load(gop_i[0:1, bass.ds(p, 1)], min_val=0, max_val=NG - 1)
                    with sp.Fori(0, EH) as e2:
                        for part in range(3):
                            for j in range(2):
                                t = p * EH + e2
                                sp.wait_ge(S("y_ps" if part == 2 else "h_ps"), t * 2 + j + 1)
                                sp.dma_start(slot[3 * j + part],
                                             A["w_exp"][bass.ds(grp * EPG + e2 * 2 + j, 1), part]
                                             .rearrange("a p n -> (a p) n")).then_inc(wfull(j, part), 16)

            @block.gpsimd
            def _(pool):
                nc.gpsimd.memset(zrow, 0.0).then_inc(S("zrow"), 1)

            @block.tensor
            def _(pe):
                pe.sem_inc(S("h_ps"), 2)
                pe.sem_inc(S("y_ps"), 2)
                pe.wait_ge(S("zrow"), 1)
                n_pass = pe.value_load(np_i[0:1, 0:1], min_val=1, max_val=MAXPASS)
                with pe.Fori(0, n_pass) as p:
                    pe.wait_ge(S("gsel_ready"), p + 1)
                    pe.wait_ge(S("hacc"), p + 1)
                    for half in range(2):
                        for k in range(4):
                            kk = 4 * half + k
                            for i in range(NT):
                                mm = nc.tensor.matmul(bank[half][:, k * P:(k + 1) * P], x2[:, i, kk * P:(kk + 1) * P],
                                                      gsel[:, i, :], start=(i == 0), stop=(i == NT - 1))
                        mm.then_inc(S("xg_ps"), 1)
                    for i in range(NT):
                        mm = nc.tensor.transpose(bank[6][:, i * P:(i + 1) * P], gsel[:, i, :], ident)
                    mm.then_inc(S("gT_ps"), 1)
                    pe.wait_ge(S("xg_sb"), p * 2 + 2)
                    for i in range(NT):
                        mm = nc.tensor.matmul(bank[7][:, 0:EPG], gsel[:, i, :], cw[:, i, :],
                                              start=(i == 0), stop=(i == NT - 1))
                    mm.then_inc(S("cwg_ps"), 1)
                    for half in range(2):
                        nc.tensor.matmul(bank[4 + half][:, :], zrow[0:1, 0:P], zrow, start=True, stop=False,
                                         skip_group_check=True)
                    with pe.Fori(0, EH) as e2:
                        t = p * EH + e2
                        for j in range(2):
                            pe.wait_ge(S("hid_ready"), t * 2 + j + 1)
                            for k in range(KT):
                                if k % 4 == 0:
                                    pe.wait_ge(wfull(j, k // 4), t * 16 + 16)
                                mm = nc.tensor.matmul(bank[j][:, :], xg[:, k, :],
                                                      slot[3 * j + k // 4][:, (k % 4) * 512:(k % 4 + 1) * 512],
                                                      start=(k == 0), stop=(k == KT - 1))
                            mm.then_inc(S("h_ps"), 1)
                        for j in range(2):
                            pe.wait_ge(S("hid_ready"), t * 2 + j + 3)
                            for f in range(2):
                                mm = nc.tensor.transpose(bank[2 + j][:, f * P:(f + 1) * P],
                                                         hid[:, j, f * P:(f + 1) * P], ident)
                            mm.then_inc(S("hT_ps"), 1)
                            pe.wait_ge(S("hT_sb"), t * 2 + j + 1)
                            pe.wait_ge(wfull(j, 2), t * 16 + 16)
                            for half in range(2):
                                for f in range(2):
                                    mm = nc.tensor.matmul(bank[4 + half][:, :], hT[:, j, f, :],
                                                          slot[3 * j + 2][:, f * DM + half * 512:f * DM + (half + 1) * 512],
                                                          start=False, stop=False, skip_group_check=True)
                            mm.then_inc(S("y_ps"), 1)
                    pe.wait_ge(S("gT_sb"), p + 1)
                    pe.wait_ge(S("yg_sb"), p * 2 + 2)
                    for i, r in enumerate(ROWS):
                        for half in range(2):
                            nc.tensor.matmul(bank[(0, 1, 2, 3, 6, 7)[2 * i + half]][:, :], gT[:, i, :],
                                             yg[:, half * 512:(half + 1) * 512],
                                             start=True, stop=True).then_inc(S("ys_ps"), 1)

            @block.scalar
            def _(act):
                n_pass = act.value_load(np_i[0:1, 0:1], min_val=1, max_val=MAXPASS)
                with act.Fori(0, n_pass) as p:
                    for half in range(2):
                        act.wait_ge(S("xg_ps"), p * 2 + half + 1)
                        nc.scalar.activation(xg[:, 4 * half:4 * half + 4, :].rearrange("p k s -> p (k s)"),
                                             bank[half][:, :], ACT.Copy).then_inc(S("xg_sb"), 1)
                    act.wait_ge(S("gT_ps"), p + 1)
                    nc.scalar.activation(gT, bank[6][:, 0:NT * P].rearrange("p (i t) -> p i t", i=NT), ACT.Copy)\
                        .then_inc(S("gT_sb"), 1)
                    with act.Fori(0, EH) as e2:
                        t = p * EH + e2
                        for j in range(2):
                            act.wait_ge(S("h_ps"), t * 2 + j + 3)
                            nc.scalar.activation(sig[:, j, :], bank[j][:, 0:FF], ACT.Sigmoid).then_inc(S("sig_ready"), 1)
                        for j in range(2):
                            act.wait_ge(S("hT_ps"), t * 2 + j + 1)
                            nc.scalar.activation(hT[:, j].rearrange("p f t -> p (f t)"), bank[2 + j][:, 0:FF], ACT.Copy)\
                                .then_inc(S("hT_sb"), 1)
                    act.wait_ge(S("y_ps"), p * EPG + EPG + 2)
                    for half in range(2):
                        nc.scalar.activation(yg[:, half * 512:(half + 1) * 512], bank[4 + half][:, :], ACT.Copy)\
                            .then_inc(S("yg_sb"), 1)

            @block.vector
            def _(dve):
                ch = Chain(dve, S("moe_dve"))
                dve.sem_inc(S("hacc"), 1)
                dve.sem_inc(S("hid_ready"), 2)
                n_pass = dve.value_load(np_i[0:1, 0:1], min_val=1, max_val=MAXPASS)
                per = 3 + 6
                dve.sem_inc(S("dest_ready"), 1)
                with dve.Fori(0, n_pass) as p:
                    ch.n, ch.at = 0, p * per
                    dve.wait_ge(S("dest_ready"), p + 1)
                    for i in range(NT):
                        ch(nc.vector.tensor_scalar(gsel[:, i, :], iot, dest[:, i:i + 1], None, ALU.is_equal))
                    dve.sem_inc(S("gsel_ready"), 1)
                    dve.wait_ge(S("cwg_ps"), p + 1)
                    nc.vector.tensor_copy(cwg, bank[7][:, 0:EPG]).then_inc(S("cwg_sb"), 1)
                    dve.wait_ge(S("cwg_sb"), p + 1)
                    nc.vector.tensor_scalar(dest, dest, float(-P), None, add).then_inc(S("dest_ready"), 1)
                    with dve.Fori(0, EH) as e2:
                        t = p * EH + e2
                        for j in range(2):
                            dve.wait_ge(S("sig_ready"), t * 2 + j + 1)
                            nc.vector.scalar_tensor_tensor(out=hid[:, j, :], in0=bank[j][:, 0:FF],
                                                           scalar=cwg[:, bass.ds(e2 * 2 + j, 1)], in1=sig[:, j, :],
                                                           op0=mult, op1=mult).then_inc(S("silu"), 1)
                            dve.wait_ge(S("silu"), t * 2 + j + 1)
                            nc.vector.tensor_tensor(hid[:, j, :], hid[:, j, :], bank[j][:, FF:2 * FF], mult)\
                                .then_inc(S("hid_ready"), 1)
                    for i, r in enumerate(ROWS):
                        for half in range(2):
                            c = slice(half * 512, (half + 1) * 512)
                            dve.wait_ge(S("ys_ps"), p * 6 + 2 * i + half + 1)
                            ch(nc.vector.tensor_tensor(h2[0:r, i, c], h2[0:r, i, c],
                                                       bank[(0, 1, 2, 3, 6, 7)[2 * i + half]][0:r, :], add))
                    dve.sem_inc(S("hacc"), 1)
                    assert ch.n == per, ch.n

        retire()

        with nc.Block("final") as block:
            @block.sync
            def _(sp):
                sp.dma_start(lnb2, ln_row[2, :].partition_broadcast(P)).then_inc(S("lnf_in"), 16)
                sp.wait_ge(S("y_ready"), 1)
                sp.dma_start(O["y_p"][0:P - NMETA, :], x2[NMETA:P, 0, :]).then_inc(S("y_out"), 16)
                sp.wait_ge(S("y_ready"), 2)
                sp.dma_start(O["y_p"][P - NMETA:2 * P - NMETA, :], x2[:, 1, :]).then_inc(S("y_out"), 16)
                sp.wait_ge(S("y_ready"), 3)
                sp.dma_start(O["y_p"][2 * P - NMETA:SEQ, :], x2[0:NMETA, 2, :]).then_inc(S("y_out"), 16)
                sp.dma_start(O["y_s"], x2[NMETA:ROWS[2], 2, :]).then_inc(S("y_out"), 16)
                sp.wait_ge(S("y_out"), 64)

            @block.scalar
            def _(act):
                for i, n in enumerate(ROWS):
                    nc.scalar.activation(jk[0:n, i, :], h2[0:n, i, :], ACT.Square,
                                         accum_out=ss[0:n, i:i + 1]).then_inc(S("ss3"), 1)
                act.wait_ge(S("ms3"), 1)
                nc.scalar.activation(rt, ms, ACT.Sqrt).then_inc(S("rt3"), 1)

            @block.vector
            def _(dve):
                ch = Chain(dve, S("final_dve"))
                dve.wait_ge(S("ss3"), 3)
                nc.vector.tensor_scalar(ms, ss, 1.0 / DM, RMS_EPS, mult, add).then_inc(S("ms3"), 1)
                dve.wait_ge(S("rt3"), 1)
                ch(nc.vector.reciprocal(rstd, rt))
                dve.wait_ge(S("lnf_in"), 16)
                for i, n in enumerate(ROWS):
                    nc.vector.scalar_tensor_tensor(out=x2[0:n, i, :], in0=h2[0:n, i, :], scalar=rstd[0:n, i:i + 1],
                                                   in1=lnb2[0:n, :], op0=mult, op1=mult).then_inc(S("y_ready"), 1)



def kernel(**inputs):
    import numpy as _np
    import concourse.bacc as _bacc
    from concourse import mybir as _mybir
    from concourse.bass_utils import run_bass_kernel_spmd as _run

    x = {k: _np.asarray(v) for k, v in inputs.items()}
    w_in = x["w_in"][0]
    w_zb = w_in[:, AP_:AP_ + 3 * BW].reshape(2, 4, P, 3, BW).transpose(3, 0, 2, 1, 4)
    w_za = w_in[:, 0:AP_].reshape(KT, P, ATILES // 2, 2 * P).transpose(2, 1, 0, 3)
    g0 = AP_ + 3 * BW + NH
    w_gate = w_in[:, g0:].reshape(KT, P, 2, DM // P, P).transpose(3, 1, 0, 2, 4)
    pa = x["proj_a"][0].reshape(4, P, DM // (2 * P), 2, P)
    pb = x["proj_b"][0].reshape(4, P, DM // (2 * P), 2, P)
    w_proj = _np.stack([pa, pb]).transpose(3, 2, 4, 0, 1, 5)
    w1 = x["exp_w1"][0].reshape(NE, KT, P, FF)
    w3 = x["exp_w3"][0].reshape(NE, KT, P, FF)
    w13 = _np.concatenate([w1, w3], 3).transpose(0, 2, 1, 3).reshape(NE, P, 2, SLOT).transpose(0, 2, 1, 3)
    w2 = x["exp_w2"][0].reshape(NE, 2, P, DM).transpose(0, 2, 1, 3).reshape(NE, 1, P, SLOT)
    rows = [x["rwkv_mu"], x["rwkv_w0"], x["rwkv_a0"], x["rwkv_k_k"], x["rwkv_k_a"], x["rwkv_r_k"],
            x["rwkv_lnx_w"], x["rwkv_lnx_b"]]
    arrays = {
        "xp": x["x_prompt"][0], "xs": x["x_sample"].reshape(NS, DM), "meta": x["meta_tokens"],
        "w_zb": w_zb.reshape(3, 2, P, SLOT), "w_za": w_za.reshape(ATILES // 2, P, SLOT),
        "w_f": w_in[:, AP_ + 3 * BW:g0].reshape(KT, P, NH).transpose(1, 0, 2),
        "w_gate": w_gate.reshape(DM // P, P, SLOT), "w_proj": w_proj.reshape(DM // (2 * P), P, SLOT),
        "w_out": x["w_out"][0].reshape(4, 2, P, DM).transpose(0, 2, 1, 3).reshape(4, P, SLOT),
        "w_exp": _np.concatenate([w13, w2], 1),
        "w_r": _np.concatenate([x["router_grp"][0], x["router_exp"][0]], 1).reshape(KT, P, NG + NE).transpose(1, 0, 2),
        "prm": _np.concatenate([r.reshape(-1, P) for r in rows]),
        "ln_rows": _np.concatenate([x["ln1_w"], x["ln2_w"], x["ln_f"][None]]),
        "lora": _np.stack([_np.concatenate([x["rwkv_w2"][0], x["rwkv_a2"][0]]), x["rwkv_g2"][0]], 1),
        "qkn": _np.concatenate([x["fox_q_norm"], x["fox_k_norm"]]), "fb": x["fox_f_bias"][0],
        "shift": x["state_shift"][0], "state": x["state_rwkv"][0],
        "pt": x["page_table"].reshape(1, DB * NPAGES),
        "ck": x["cache_k"][0].reshape(-1, PAGE, BW), "cv": x["cache_v"][0].reshape(-1, PAGE, BW),
        "clf": x["cache_logf"][0].reshape(-1, PAGE * NH),
    }
    outs = {
        "y_p": (SEQ, DM), "y_s": (NS, DM), "k_p": (LP, BW), "v_p": (LP, BW), "lf_p": (LP, NH),
        "rw_p": (NH, HD, HD), "shift_p": (1, AP_), "k_s": (NS, BW), "v_s": (NS, BW), "lf_s": (NS, NH),
        "rw_s": (DB, NH, HD, HD), "shift_s": (DB, AP_),
    }
    nc = _bacc.Bacc("TRN2", target_bir_lowering=False, num_devices=1)
    A, O, maps = {}, {}, {}
    for n, a in arrays.items():
        a = _np.ascontiguousarray(a)
        maps["in_" + n] = a
        A[n] = nc.dram_tensor("in_" + n, a.shape, _mybir.dt.from_np(a.dtype), kind="ExternalInput").ap()
    for n, s in outs.items():
        O[n] = nc.dram_tensor("out_" + n, s, _mybir.dt.float32, kind="ExternalOutput").ap()
    A["cn_dram"] = nc.dram_tensor("cn_dram", (NS, NH), _mybir.dt.float32, kind="Internal").ap()
    build(nc, A, O)
    r = _run(nc, [maps], core_ids=[0]).results[0]
    g = {n: r["out_" + n] for n in outs}
    kv = (1, 1, LP, NH, HD)
    kvs = (1, DB, DS, NH, HD)
    return (g["y_p"].reshape(1, SEQ, DM), g["y_s"].reshape(DB, DS, DM), g["k_p"].reshape(kv), g["v_p"].reshape(kv),
            g["lf_p"].reshape(1, 1, LP, NH), g["rw_p"].reshape(1, 1, NH, HD, HD), g["shift_p"].reshape(1, 1, AP_),
            g["k_s"].reshape(kvs), g["v_s"].reshape(kvs), g["lf_s"].reshape(1, DB, DS, NH),
            g["rw_s"].reshape(1, DB, NH, HD, HD), g["shift_s"].reshape(1, DB, AP_))
```
